# Optimizing a Trainium2 kernel written in Bass

```python
import math
import jax, jax.numpy as jnp
from jax import lax
import numpy as np

D_MODEL = 2048
BATCH = 1
SEQ = 1024
DEPTH = 1

CHUNK = 64
HEAD_DIM = 64
N_HEADS = 16
N_KV_HEADS = 2
GROUP = N_HEADS // N_KV_HEADS
ATTN_WIDTH = N_HEADS * HEAD_DIM
KV_WIDTH = N_KV_HEADS * HEAD_DIM
WINDOW = 128
WINDOW_CHUNKS = WINDOW // CHUNK
BAND = WINDOW_CHUNKS * CHUNK
N_BUCKETS = 32
MAX_DISTANCE = 128
CONV_WIDTH = D_MODEL // 2
CONV_K = 3
D_MIX = ATTN_WIDTH + CONV_WIDTH
SPLIT_SIZES = (ATTN_WIDTH, KV_WIDTH, KV_WIDTH, ATTN_WIDTH,
               CONV_WIDTH, CONV_WIDTH, CONV_WIDTH, CONV_WIDTH)
SPLIT_POINTS = tuple(int(s) for s in np.cumsum(SPLIT_SIZES)[:-1])
IN_COLS = int(sum(SPLIT_SIZES))
EPS = 1e-6
NEG = -1e30

kernel_name = "hymba_swa_sink_shortconv_t5bias"

def rmsnorm(x, w):
    xf = x.astype(jnp.float32)
    y = xf * lax.rsqrt(jnp.mean(xf * xf, axis=-1, keepdims=True) + EPS)
    return (y * w.astype(jnp.float32)).astype(x.dtype)

def t5_bucket(rel):
    n = -rel
    half = N_BUCKETS // 2
    ret = (n < 0).astype(np.int32) * half
    n = np.abs(n)
    max_exact = half // 2
    nf = np.maximum(n, 1).astype(np.float32)
    large = max_exact + (np.log(nf / max_exact) / math.log(MAX_DISTANCE / max_exact)
                         * (half - max_exact)).astype(np.int32)
    large = np.minimum(large, half - 1)
    return ret + np.where(n < max_exact, n, large).astype(np.int32)

def band_bias(rel_bias):
    i = np.arange(CHUNK)[:, None]
    j = np.arange(BAND)[None, :]
    rel = j - (WINDOW_CHUNKS - 1) * CHUNK - i
    bucket = jnp.asarray(t5_bucket(rel))
    b = jnp.take(rel_bias.astype(jnp.float32), bucket, axis=0)
    return jnp.transpose(b, (2, 0, 1)).reshape(N_KV_HEADS, GROUP, CHUNK, BAND)

def make_band(t):
    parts = []
    for s in reversed(range(WINDOW_CHUNKS)):
        if s == 0:
            parts.append(t)
        else:
            pad = [(0, 0)] * t.ndim
            pad[1] = (s, 0)
            parts.append(jnp.pad(t, pad)[:, :-s])
    return jnp.concatenate(parts, axis=2)

def swa_sink_attention(q, k, v, sinks, rel_bias):
    b_, s_, _ = q.shape
    nc = s_ // CHUNK
    q = q.reshape(b_, nc, CHUNK, N_KV_HEADS, GROUP, HEAD_DIM)
    kb = make_band(k.reshape(b_, nc, CHUNK, N_KV_HEADS, HEAD_DIM))
    vb = make_band(v.reshape(b_, nc, CHUNK, N_KV_HEADS, HEAD_DIM))
    logits = jnp.einsum('bnqkgd,bnskd->bnkgqs', q, kb).astype(jnp.float32)
    logits = logits * (1.0 / math.sqrt(HEAD_DIM)) + band_bias(rel_bias)[None, None]
    key_back = (WINDOW_CHUNKS - 1) - jnp.arange(BAND) // CHUNK
    valid = jnp.arange(nc)[:, None] >= key_back[None, :]
    logits = jnp.where(valid[None, :, None, None, None, :], logits, NEG)
    sink = sinks.astype(jnp.float32).reshape(1, 1, N_KV_HEADS, GROUP, 1, 1)
    m = jnp.maximum(jnp.max(logits, axis=-1, keepdims=True), sink)
    p = jnp.exp(logits - m)
    denom = jnp.sum(p, axis=-1, keepdims=True) + jnp.exp(sink - m)
    p = (p / denom).astype(vb.dtype)
    o = jnp.einsum('bnkgqs,bnskd->bnqkgd', p, vb)
    return o.reshape(b_, s_, ATTN_WIDTH)

def short_gated_conv(h, c_gate, b_gate, conv_w, conv_b):
    u = c_gate * h
    up = jnp.pad(u, ((0, 0), (CONV_K - 1, 0), (0, 0)))
    s_ = u.shape[1]
    y = conv_b
    for t in range(CONV_K):
        y = y + conv_w[t] * up[:, t:t + s_]
    return b_gate * y

def setup_inputs(seed: int = 0) -> dict:
    key = jax.random.key(seed)
    ks = jax.random.split(key, 9)
    f32 = jnp.float32
    x = jax.random.normal(ks[0], (BATCH, SEQ, D_MODEL), f32)
    norm_w = 1.0 + 0.02 * jax.random.normal(ks[1], (DEPTH, D_MODEL), f32)
    w_in = jax.random.normal(ks[2], (DEPTH, D_MODEL, IN_COLS), f32) * D_MODEL ** -0.5
    sinks = jax.random.normal(ks[3], (DEPTH, N_HEADS), f32)
    conv_w = jax.random.normal(ks[4], (DEPTH, CONV_K, CONV_WIDTH), f32) * CONV_K ** -0.5
    conv_b = 0.01 * jax.random.normal(ks[5], (DEPTH, CONV_WIDTH), f32)
    w_out = jax.random.normal(ks[6], (DEPTH, D_MIX, D_MODEL), f32) * D_MIX ** -0.5
    rel_bias = 0.5 * jax.random.normal(ks[7], (N_BUCKETS, N_HEADS), f32)
    final_norm_w = 1.0 + 0.02 * jax.random.normal(ks[8], (D_MODEL,), f32)
    return {"x": x, "norm_w": norm_w, "w_in": w_in, "sinks": sinks,
            "conv_w": conv_w, "conv_b": conv_b, "w_out": w_out,
            "rel_bias": rel_bias, "final_norm_w": final_norm_w}

def reference(x, norm_w, w_in, sinks, conv_w, conv_b, w_out, rel_bias, final_norm_w):
    for l in range(DEPTH):
        hn = rmsnorm(x, norm_w[l])
        proj = jnp.einsum('bsd,de->bse', hn, w_in[l])
        q, k, v, g_attn, h, c_gate, b_gate, g_conv = jnp.split(proj, SPLIT_POINTS, axis=-1)
        attn = swa_sink_attention(q, k, v, sinks[l], rel_bias)
        conv = short_gated_conv(h, c_gate, b_gate, conv_w[l], conv_b[l])
        mixed = jnp.concatenate([attn * jax.nn.silu(g_attn),
                                 conv * jax.nn.silu(g_conv)], axis=-1)
        x = x + jnp.einsum('bse,ed->bsd', mixed, w_out[l])
    return rmsnorm(x, final_norm_w)


_drawn_inputs = setup_inputs


def setup_inputs(seed=0):
    import zlib

    import numpy as np

    out = dict(_drawn_inputs(seed))
    spreads = {}
    factors = {'norm_w': 3.449, 'sinks': 64.0, 'conv_b': 61.587, 'final_norm_w': 8.186, 'rel_bias': 5.706}
    for name, (base, spread) in spreads.items():
        noise = np.random.default_rng([zlib.crc32(name.encode()), seed]).standard_normal(out[name].shape)
        drawn = base * np.exp(spread * noise) if base else spread * noise
        out[name] = __import__('jax').numpy.asarray(drawn.astype(out[name].dtype))
    for name, factor in factors.items():
        out[name] = (out[name] * factor).astype(out[name].dtype)
    return out
```

```python
import math
from contextlib import ExitStack

import numpy as np
import concourse.bass as bass
from concourse import mybir

F32 = mybir.dt.float32
F32R = mybir.dt.float32r
ALU = mybir.AluOpType
ACT = mybir.ActivationFunctionType
AX_X = mybir.AxisListType.X

P = 128
D = 2048
S = 1024
CHUNK = 64
HEAD = 64
BAND = 2 * CHUNK
HEADS = 16
KVH = 2
PAIRS = HEADS // KVH // 2
ATTN = HEADS * HEAD
CONV = 1024
TAPS = 3
IN_COLS = 2 * ATTN + 2 * KVH * HEAD + 4 * CONV
BUCKETS = 32
MAX_DISTANCE = 128
EPS = 1e-6
NEG = -1e30
SCALE = 1.0 / math.sqrt(HEAD)

KT = D // P
QK = KT // 4
ST = S // P
NC = S // CHUNK
N = 512
SH = S // N
QKV_TILES = (ATTN + 2 * KVH * HEAD) // P
K_ROW = ATTN
V_ROW = ATTN + KVH * HEAD
A_TILES = QKV_TILES + ATTN // P
GROUPS = CONV // P
TILES = A_TILES + 4 * GROUPS
UNITS = NC * KVH
REL = 192
BLOCKS = SH * (D // N)
WO_Q = 4 * TILES


def t5_one_hot():
    rel = np.arange(REL) - (BAND - 1)
    n = -rel
    half = BUCKETS // 2
    ret = (n < 0).astype(np.int32) * half
    n = np.abs(n)
    max_exact = half // 2
    nf = np.maximum(n, 1).astype(np.float32)
    large = max_exact + (np.log(nf / max_exact) / math.log(MAX_DISTANCE / max_exact)
                         * (half - max_exact)).astype(np.int32)
    large = np.minimum(large, half - 1)
    bucket = ret + np.where(n < max_exact, n, large).astype(np.int32)
    return (bucket[None, :] == np.arange(BUCKETS)[:, None]).astype(np.float32)


def build(nc, x, norm_w, w_in, sinks, conv_w, conv_b, w_out, rel_bias, final_norm_w, one_hot, out):
    ctx = ExitStack()
    with ctx:
        def sb(name, shape, dt=F32):
            return ctx.enter_context(nc.sbuf_tensor(name, shape, dt))

        def sem(name):
            return ctx.enter_context(nc.semaphore(name))

        qkv_park = nc.dram_tensor("qkv_park", [2, QKV_TILES * P, CHUNK + S], F32, kind="Internal").ap()
        gate_park = nc.dram_tensor("gate_park", [ATTN, S], F32, kind="Internal").ap()
        mix_park = nc.dram_tensor("mix_park", [ATTN + CONV, S], F32, kind="Internal").ap()
        rel_park = nc.dram_tensor("rel_park", [HEADS, CHUNK, REL], F32, kind="Internal").ap()

        act_hi = sb("act_hi", [P, KT, S], F32R)
        act_lo = sb("act_lo", [P, KT, S], F32R)
        w_raw = sb("w_raw", [P, 4, N])
        w_hi = sb("w_hi", [P, 4, N], F32R)
        w_lo = sb("w_lo", [P, 4, N], F32R)
        q_cur = sb("q_cur", [P, PAIRS * 2, CHUNK], F32R)
        k_cur = sb("k_cur", [P, 2, BAND], F32R)
        pt_hi = sb("pt_hi", [P, N], F32R)
        pt_lo = sb("pt_lo", [P, N], F32R)
        v_cur = sb("v_cur", [P, 2, KVH, 2, HEAD], F32R)
        ident = sb("ident", [P, P])
        taps = sb("taps", [P, TAPS + 1, GROUPS])
        small = sb("small", [P, 68])
        ssq = sb("ssq", [P, 4, 4])

        arena = sb("arena", [P, 4 * D])
        stage = sb("stage", [P, 2, S])
        resid = sb("resid", [P, 2, N])

        off = [0]

        def carve(n):
            off[0] += n
            return arena[:, off[0] - n:off[0]]

        h_buf = carve(S)
        u_buf = carve(2 + S)
        y_buf = carve(S)
        bias = carve(HEADS // 2 * BAND).rearrange("p (j k) -> p j k", j=HEADS // 2)
        LW = BAND + 1
        logits = [carve(PAIRS * LW).rearrange("p (j k) -> p j k", j=PAIRS) for _ in range(KVH)]
        probs = carve(PAIRS * LW).rearrange("p (j k) -> p j k", j=PAIRS)
        v_win = carve(2 * BAND).rearrange("p (c k) -> p c k", c=2)
        g_cur = carve(PAIRS * CHUNK).rearrange("p (j k) -> p j k", j=PAIRS)
        o_mix = carve(PAIRS * CHUNK).rearrange("p (j k) -> p j k", j=PAIRS)
        assert off[0] <= 4 * D
        x_tile = [arena[:, 0:D], arena[:, D:2 * D]]
        norm_row = arena[:, 2 * D:3 * D]
        square = arena[:, 3 * D:4 * D]
        tap_rows = stage[0:(TAPS + 1) * GROUPS, 0, 0:P]
        rel_rows = stage[0:BUCKETS, 0, P:P + HEADS]
        hot_rows = stage[0:BUCKETS, 0, 256:256 + REL]
        rel_tab = stage[0:HEADS, 0, 512:512 + REL]
        zeros = stage[:, 0, 768:768 + CHUNK]
        y_res = arena[:, :].rearrange("p (t c) -> p t c", t=4)
        final_row = stage[:, :, :].rearrange("p a s -> p (a s)")

        row_max = small[:, 0:4]
        row_sum = small[:, 4:8]
        row_inv = small[:, 8:12]
        minus_half = small[:, 64:68]
        x_ssq = small[:, 12:20]
        x_var = small[:, 20:28]
        x_rstd = small[:, 28:36]
        y_ssq = small[:, 36:40]
        y_var = small[:, 40:44]
        y_rstd = small[:, 44:48]
        sink_row = small[:, 48:64]

        banks = ctx.enter_context(nc.psum_tensor("banks", [P, 8, N], F32))
        proj = [banks[:, 0:2, :], banks[:, 2:4, :]]
        v_ps, logit_ps, pt_ps, o_ps = (banks[:, b, :] for b in range(4, 8))

        ident_zero = sem("ident_zero")
        minus_half_ready = sem("minus_half_ready")
        ident_ready = sem("ident_ready")
        small_loaded = sem("small_loaded")
        u_zeroed = sem("u_zeroed")
        zeros_ready = sem("zeros_ready")
        pad_stored = sem("pad_stored")
        taps_turned = sem("taps_turned")
        rel_looked_up = sem("rel_looked_up")
        rel_copied = sem("rel_copied")
        rel_stored = sem("rel_stored")
        bias_loaded = sem("bias_loaded")
        neg_written = sem("neg_written")
        sinks_placed = sem("sinks_placed")
        norm_row_loaded = sem("norm_row_loaded")
        x_loaded = [sem(f"x_loaded{i}") for i in range(2)]
        x_squared = sem("x_squared")
        x_var_ready = sem("x_var_ready")
        x_rstd_ready = sem("x_rstd_ready")
        x_normed = sem("x_normed")
        x_turned = sem("x_turned")
        hn_hi_ready = sem("hn_hi_ready")
        hn_lo_ready = sem("hn_lo_ready")
        raw_loaded = [sem(f"raw_loaded{i}") for i in range(4)]
        w_hi_ready = sem("w_hi_ready")
        w_lo_ready = sem("w_lo_ready")
        w_free = sem("w_free")
        proj_free = sem("proj_free")
        hi_staged = sem("hi_staged")
        qkv_stored = sem("qkv_stored")
        gate_exp = sem("gate_exp")
        gate_divisor = sem("gate_divisor")
        sigmoid_ready = sem("sigmoid_ready")
        gate_stored = sem("gate_stored")
        conv_step = sem("conv_step")
        conv_out = sem("conv_out")
        conv_stored = sem("conv_stored")
        qk_loaded = sem("qk_loaded")
        v_loaded = sem("v_loaded")
        g_loaded = sem("g_loaded")
        qk_done = sem("qk_done")
        logits_read = sem("logits_read")
        max_ready = sem("max_ready")
        shifted = sem("shifted")
        exp_done = sem("exp_done")
        sum_ready = sem("sum_ready")
        inv_ready = sem("inv_ready")
        probs_ready = sem("probs_ready")
        probs_turned = sem("probs_turned")
        pt_hi_ready = sem("pt_hi_ready")
        pt_lo_ready = sem("pt_lo_ready")
        v_turned = sem("v_turned")
        v_ready = sem("v_ready")
        pv_done = sem("pv_done")
        o_ready = sem("o_ready")
        o_stored = sem("o_stored")
        mix_loaded = [sem(f"mix_loaded{i}") for i in range(2)]
        mix_hi_ready = sem("mix_hi_ready")
        mix_lo_ready = sem("mix_lo_ready")
        out_done = sem("out_done")
        bank_free = sem("bank_free")
        resid_loaded = [sem(f"resid_loaded{i}") for i in range(2)]
        y_ready = sem("y_ready")
        y_ssq_ready = sem("y_ssq_ready")
        y_var_ready = sem("y_var_ready")
        y_rstd_ready = sem("y_rstd_ready")
        final_row_loaded = sem("final_row_loaded")
        y_final = sem("y_final")
        out_stored = sem("out_stored")

        w_in_v = w_in[0].rearrange("(k p) c -> p k c", p=P)
        w_out_v = w_out[0].rearrange("(k p) c -> p k c", p=P)
        x_v = x[0].rearrange("(t p) d -> p t d", p=P)
        out_v = out[0].rearrange("(t p) d -> p t d", p=P)
        qkv_v = qkv_park.rearrange("c (m p) s -> p c m s", p=P)
        qkv_head = qkv_park.rearrange("c (h d) s -> d c h s", d=HEAD)
        gate_v = gate_park.rearrange("(m p) s -> p m s", p=P)
        mix_v = mix_park.rearrange("(m p) s -> p m s", p=P)

        def mix_row_tile(t):
            return (t + ATTN // P) % KT

        def conv_col(kind, g):
            return A_TILES * P + kind * CONV + g * P

        block = ctx.enter_context(nc.Block())

        @block.sync
        def _(sp):
            def at(column):
                return column if isinstance(column, int) else sp.snap(column)

            def load_in(slot, quarter, col):
                col = at(col)
                if not (isinstance(quarter, int) and quarter < 4):
                    sp.wait_ge(w_lo_ready, quarter - 3)
                sp.dma_start(w_raw[:, slot, :].rearrange("p (k c) -> p k c", k=QK),
                             w_in_v[:, slot * QK:(slot + 1) * QK, bass.ds(col, P)]
                             ).then_inc(raw_loaded[slot], 16)

            def load_out(slot, piece, row_tile, dblk):
                sp.wait_ge(w_lo_ready, WO_Q + piece - 3)
                sp.dma_start(w_raw[:, slot, :], w_out_v[:, row_tile, dblk * N:(dblk + 1) * N]
                             ).then_inc(raw_loaded[slot], 16)

            def load_qk(queries, band, kv):
                for c in range(2):
                    half = slice(c * HEAD, (c + 1) * HEAD)
                    sp.dma_start(q_cur[half, :, :].bitcast(F32),
                                 qkv_head[:, c, kv * PAIRS * 2:(kv + 1) * PAIRS * 2,
                                          bass.ds(queries, CHUNK)]).then_inc(qk_loaded, 16)
                    sp.dma_start(k_cur[half, :, :].bitcast(F32),
                                 qkv_head[:, :, K_ROW // HEAD + kv, bass.ds(band, BAND)]
                                 ).then_inc(qk_loaded, 16)

            def load_v(band):
                sp.dma_start(v_win, qkv_v[:, :, V_ROW // P, bass.ds(band, BAND)]).then_inc(v_loaded, 16)

            def load_mix(t):
                if t >= 2:
                    sp.wait_ge(mix_lo_ready, t - 1)
                if t < GROUPS:
                    sp.wait_ge(conv_stored, 16 * (t + 1))
                else:
                    sp.wait_ge(o_stored, 16 * UNITS)
                sp.dma_start(stage[:, t % 2, :], mix_v[:, mix_row_tile(t), :]).then_inc(mix_loaded[t % 2], 16)

            sp.dma_start(x_tile[0], x_v[:, 0, :]).then_inc(x_loaded[0], 16)
            sp.dma_start(norm_row, bass.AP(tensor=norm_w.tensor, offset=0, ap=[[0, P], [1, D]])
                         ).then_inc(norm_row_loaded, 16)
            sp.dma_start(x_tile[1], x_v[:, 1, :]).then_inc(x_loaded[1], 16)
            for q in range(4):
                load_in(q, q, 0)
            for t in range(2, ST):
                sp.wait_ge(x_turned, 4 * (t - 1))
                sp.dma_start(x_tile[t % 2], x_v[:, t, :]).then_inc(x_loaded[t % 2], 16)
            for q in range(3):
                load_in(q, 4 + q, P)
            sp.wait_ge(rel_stored, 16)
            sp.wait_ge(hn_lo_ready, 4 * ST)
            for par in range(2):
                sp.dma_start(bias[par * CHUNK:(par + 1) * CHUNK, :, :],
                             bass.AP(tensor=rel_park.tensor, offset=par * CHUNK * REL + CHUNK - 1,
                                     ap=[[REL - 1, CHUNK], [2 * CHUNK * REL, HEADS // 2], [1, BAND]])
                             ).then_inc(bias_loaded, 16)

            with sp.Fori(0, A_TILES - 1) as e:
                load_in(3, e * 4 + 7, e * P + P)
                for q in range(3):
                    load_in(q, e * 4 + 8 + q, e * P + 2 * P)
            e = A_TILES - 1
            load_in(3, 4 * e + 7, conv_col(0, 0))
            for q in range(3):
                load_in(q, 4 * e + 8 + q, conv_col(1, 0))
            sp.wait_ge(qkv_stored, 32 * QKV_TILES)
            sp.wait_ge(pad_stored, 64)
            load_qk(CHUNK, 0, 0)
            load_v(0)
            def group(g, last):
                for kind in range(4):
                    e = g * 4 + A_TILES + kind
                    unit = g * 4 + kind
                    if not (last and kind == 3):
                        band = at((g * 2 + (kind + 1) // 2) * CHUNK)
                        queries = at((g * 2 + (kind + 1) // 2) * CHUNK + CHUNK)
                        sp.wait_ge(qk_done, unit + 1)
                        load_qk(queries, band, (kind + 1) % 2)

                    def raw(k):
                        ahead = kind + (1 if k == 0 else 2)
                        slot = (3 + k) % 4
                        if last and ahead >= 4:
                            piece = 4 * (ahead - 4) + slot
                            load_out(slot, piece, mix_row_tile(piece), 0)
                        else:
                            load_in(slot, e * 4 + 7 + k, conv_col(ahead % 4, g + ahead // 4))

                    raw(0)
                    raw(1)
                    if kind % 2 == 0 and not (last and kind == 2):
                        band = at((g * 2 + kind // 2 + 1) * CHUNK)
                        sp.wait_ge(v_turned, g * 2 + kind // 2 + 1)
                        load_v(band)
                    if last and kind == 3:
                        load_mix(0)
                        load_mix(1)
                    raw(2)
                    raw(3)

            group(0, False)
            with sp.Fori(1, GROUPS - 1) as g:
                group(g, False)
            group(GROUPS - 1, True)

            load_mix(2)
            load_mix(3)

            def load_resid(r):
                half, dblk, st = r // 16, r // 4 % 4, r % 4
                if r >= 2:
                    sp.wait_ge(y_ready, r - 1)
                sp.dma_start(resid[:, r % 2, :], x_v[:, half * 4 + st, dblk * N:(dblk + 1) * N]
                             ).then_inc(resid_loaded[r % 2], 16)

            for b in range(BLOCKS):
                for k in range(KT):
                    piece = b * KT + k
                    ahead = piece + 7
                    if b > 0 and k in (2, 3):
                        load_resid(4 * b - 4 + k)
                    if ahead < BLOCKS * KT:
                        load_out(ahead % 4, ahead, mix_row_tile(ahead % KT), ahead // KT % 4)
                    if b == 0 and k + 4 < KT:
                        load_mix(k + 4)
                    if k == KT - 2:
                        load_resid(4 * b)
                        load_resid(4 * b + 1)
                if b == 0:
                    sp.wait_ge(mix_lo_ready, KT)
                    sp.dma_start(final_row, bass.AP(tensor=final_norm_w.tensor, offset=0, ap=[[0, P], [1, D]])
                                 ).then_inc(final_row_loaded, 16)
            load_resid(4 * BLOCKS - 2)
            load_resid(4 * BLOCKS - 1)
            sp.wait_ge(out_stored, 16 * ST)

        @block.gpsimd
        def _(pool):
            pool.sem_inc(w_free, 4)
            pool.sem_inc(proj_free, 2)
            pool.sem_inc(bank_free, 8)
            pool.memset(ident[:, :], 0.0).then_inc(ident_zero, 1)
            pool.memset(minus_half, -0.5).then_inc(minus_half_ready, 1)
            pool.wait_ge(ident_zero, 1)
            pool.affine_select(out=ident[:, :], in_=ident[:, :], compare_op=ALU.not_equal, fill=1.0, base=0,
                               pattern=[[-1, P]], channel_multiplier=1).then_inc(ident_ready, 1)
            for t in range(TAPS):
                pool.dma_start(tap_rows[t * GROUPS:(t + 1) * GROUPS, :],
                               conv_w[0, t].rearrange("(g p) -> g p", p=P)).then_inc(small_loaded, 16)
            pool.dma_start(tap_rows[TAPS * GROUPS:, :],
                           conv_b[0].rearrange("(g p) -> g p", p=P)).then_inc(small_loaded, 16)
            pool.dma_start(rel_rows, rel_bias).then_inc(small_loaded, 16)
            pool.dma_start(hot_rows, one_hot).then_inc(small_loaded, 16)
            pool.dma_start(sink_row, bass.AP(tensor=sinks.tensor, offset=0, ap=[[0, P], [1, HEADS]])
                           ).then_inc(small_loaded, 16)
            pool.wait_ge(zeros_ready, 1)
            for c in range(2):
                for m in (K_ROW // P, V_ROW // P):
                    pool.dma_start(qkv_v[:, c, m, 0:CHUNK], zeros).then_inc(pad_stored, 16)
            pool.wait_ge(minus_half_ready, 1)
            for t in range(ST):
                pool.wait_ge(x_var_ready, t + 1)
                pool.tensor_tensor(x_rstd[:, t:t + 1], x_var[:, t:t + 1], minus_half[:, 0:1], ALU.pow
                                   ).then_inc(x_rstd_ready, 1)
            pool.wait_ge(rel_copied, 1)
            pool.dma_start(rel_park, rel_tab.unsqueeze(1).to_broadcast([HEADS, CHUNK, REL])).then_inc(rel_stored, 16)

            with pool.Fori(0, QKV_TILES) as m:
                pool.wait_ge(proj_free, m + 3)
                for c in range(2):
                    pool.dma_start(qkv_v[:, c, bass.ds(m, 1), CHUNK:].rearrange("p a s -> p (a s)"),
                                   stage[:, c, :]).then_inc(qkv_stored, 16)
            with pool.Fori(0, A_TILES - QKV_TILES) as m:
                pool.wait_ge(proj_free, m + (QKV_TILES + 3))
                pool.dma_start(gate_v[:, bass.ds(m, 1), :].rearrange("p a s -> p (a s)"), y_buf
                               ).then_inc(gate_stored, 16)
            with pool.Fori(0, GROUPS) as g:
                for kind in range(4):
                    pool.wait_ge(o_ready, g * 4 + kind + 1)
                    pool.dma_start(mix_v[:, (kind % 2) * PAIRS:(kind % 2 + 1) * PAIRS,
                                         bass.ds((g * 2 + kind // 2) * CHUNK, CHUNK)], o_mix
                                   ).then_inc(o_stored, 16)
                pool.wait_ge(conv_out, g + 1)
                pool.dma_start(mix_v[:, bass.ds(g + ATTN // P, 1), :].rearrange("p a s -> p (a s)"), y_buf
                               ).then_inc(conv_stored, 16)
            for t in range(ST):
                if t % 4 == 0:
                    pool.wait_ge(y_var_ready, t // 4 + 1)
                    pool.tensor_tensor(y_rstd, y_var, minus_half, ALU.pow).then_inc(y_rstd_ready, 1)
                pool.wait_ge(y_final, 4 * (t + 1))
                pool.dma_start(out_v[:, t, :], y_res[:, t % 4, :]).then_inc(out_stored, 16)

        @block.scalar
        def _(act):
            def split(slot, quarter, turn):
                act.wait_ge(raw_loaded[slot], turn * 16 + 16)
                act.wait_ge(w_free, quarter + 1)
                act.activation(w_hi[:, slot, :], w_raw[:, slot, :], ACT.Copy).then_inc(w_hi_ready, 1)

            def square_x(t):
                act.wait_ge(x_loaded[t % 2], 16 * (t // 2 + 1))
                if t >= 1:
                    act.wait_ge(x_squared, t)
                act.activation(square, x_tile[t % 2], ACT.Square, accum_out=x_ssq[:, t:t + 1]
                               ).then_inc(x_squared, 1)

            square_x(0)
            for t in range(ST):
                if t + 1 < ST:
                    square_x(t + 1)
                for b in range(4):
                    act.wait_ge(x_turned, 4 * t + b + 1)
                    act.activation(act_hi[:, 4 * b:4 * b + 4, t * P:(t + 1) * P],
                                   banks[:, (t % 2) * 4 + b, :].rearrange("p (k s) -> p k s", k=4), ACT.Copy
                                   ).then_inc(hn_hi_ready, 1)
            for q in range(3):
                split(q, q, 0)

            act.wait_ge(rel_stored, 16)
            act.wait_ge(pad_stored, 64)
            def stage_hi(e, par, first):
                act.wait_ge(w_free, e * 4 + 8)
                if not first:
                    act.wait_ge(qkv_stored, e * 32)
                act.activation(stage[:, 0, :].bitcast(F32R).rearrange("p (a s) -> p a s", a=2),
                               proj[par], ACT.Copy).then_inc(hi_staged, 1)

            def exp_gate(tile, par):
                act.wait_ge(w_free, tile * 4 + 8)
                act.wait_ge(proj_free, tile + 2)
                act.activation(h_buf.rearrange("p (a s) -> p a s", a=2), proj[par], ACT.Exp, scale=-1.0
                               ).then_inc(gate_exp, 1)

            def splits(e, middle=None):
                split(3, e * 4 + 3, e)
                if middle:
                    middle()
                for q in range(3):
                    split(q, e * 4 + 4 + q, e + 1)

            def qkv_pair(i, first):
                for par in range(2):
                    splits(i * 2 + (1 + par), lambda: stage_hi(i * 2 + par, par, first and par == 0))

            splits(0)
            qkv_pair(0, True)
            with act.Fori(1, QKV_TILES // 2) as i:
                qkv_pair(i, False)
            with act.Fori(QKV_TILES // 2, A_TILES // 2 - 1) as i:
                for par in range(2):
                    splits(i * 2 + (1 + par), lambda: exp_gate(i * 2 + par, par))
            splits(A_TILES - 1, lambda: exp_gate(A_TILES - 2, 0))

            def group(g, last):
                for kind in range(4):
                    e = g * 4 + A_TILES + kind
                    unit = g * 4 + kind
                    act.wait_ge(shifted, unit + 1)
                    act.activation(probs, probs, ACT.Exp).then_inc(exp_done, 1)
                    split(3, e * 4 + 3, e)
                    if kind == 0:
                        exp_gate(e - 1, 1)
                    split(0, e * 4 + 4, e + 1)
                    if kind % 2 == 0:
                        n = g * 2 + kind // 2
                        act.wait_ge(v_turned, n + 1)
                        for c in range(2):
                            v_in = v_ps[:, c * P:(c + 1) * P].rearrange("p (h d) -> p h d", h=KVH)
                            for copy in range(2):
                                op = act.activation(v_cur[:, c, :, copy, :], v_in, ACT.Copy)
                        op.then_inc(v_ready, 1)
                    act.wait_ge(probs_turned, unit + 1)
                    act.activation(pt_hi[:, :], pt_ps, ACT.Copy).then_inc(pt_hi_ready, 1)
                    if isinstance(g, int) and g == 0 and kind == 0:
                        act.wait_ge(gate_stored, 16 * (A_TILES - QKV_TILES))
                    act.dma_start(g_cur, gate_v[:, (kind % 2) * PAIRS:(kind % 2 + 1) * PAIRS,
                                                bass.ds((g * 2 + kind // 2) * CHUNK, CHUNK)]
                                  ).then_inc(g_loaded, 16)
                    split(1, e * 4 + 5, e + 1)
                    if last and kind == 3:
                        mix_hi(0)
                    split(2, e * 4 + 6, e + 1)
                    if last and kind == 3:
                        mix_hi(1)

            def mix_hi(t):
                act.wait_ge(mix_loaded[t % 2], 16 * (t // 2 + 1))
                act.wait_ge(w_free, 4 * TILES + t // 4 + 1)
                act.activation(act_hi[:, t, :], stage[:, t % 2, :], ACT.Copy).then_inc(mix_hi_ready, 1)

            group(0, False)
            with act.Fori(1, GROUPS - 1) as g:
                group(g, False)
            group(GROUPS - 1, True)

            mix_hi(2)
            exp_gate(TILES - 1, 1)
            mix_hi(3)

            def square_y(r):
                act.wait_ge(y_ready, r + 1)
                b, st = r // 4, r % 4
                act.activation(banks[:, 4 - 4 * (b % 2) + st, :], y_res[:, st, (b % 4) * N:(b % 4 + 1) * N],
                               ACT.Square, accum_out=ssq[:, st, b % 4:b % 4 + 1]).then_inc(bank_free, 1)

            for b in range(BLOCKS):
                for k in range(KT):
                    piece = b * KT + k + 3
                    if piece < BLOCKS * KT:
                        split(piece % 4, WO_Q + piece, TILES + piece // 4)
                    if b == 0 and k + 4 < KT:
                        mix_hi(k + 4)
                    if b > 0 and k < 4:
                        square_y(4 * (b - 1) + k)
            for st in range(4):
                square_y(4 * (BLOCKS - 1) + st)

        @block.vector
        def _(dve):
            def split(quarter, slot):
                dve.wait_ge(w_hi_ready, quarter + 1)
                dve.tensor_tensor(w_lo[:, slot, :], w_raw[:, slot, :], w_hi[:, slot, :], ALU.subtract
                                  ).then_inc(w_lo_ready, 1)

            dve.memset(zeros, 0.0).then_inc(zeros_ready, 1)
            dve.wait_ge(taps_turned, 1)
            dve.tensor_copy(taps[:, :, :].rearrange("p t g -> p (t g)"), banks[:, 7, 0:(TAPS + 1) * GROUPS]
                            ).then_inc(rel_looked_up, 1)
            dve.wait_ge(taps_turned, 2)
            dve.tensor_copy(rel_tab, banks[0:HEADS, 6, 0:REL]).then_inc(rel_copied, 1)
            dve.wait_ge(norm_row_loaded, 16)

            def normalise_x(t):
                dve.wait_ge(x_squared, t + 1)
                dve.tensor_scalar(x_var[:, t:t + 1], x_ssq[:, t:t + 1], 1.0 / D, EPS, ALU.mult, ALU.add
                                  ).then_inc(x_var_ready, 1)
                dve.wait_ge(x_rstd_ready, t + 1)
                dve.scalar_tensor_tensor(out=x_tile[t % 2], in0=x_tile[t % 2], scalar=x_rstd[:, t:t + 1],
                                         in1=norm_row, op0=ALU.mult, op1=ALU.mult).then_inc(x_normed, 1)

            normalise_x(0)
            for t in range(ST):
                if t + 1 < ST:
                    normalise_x(t + 1)
                for b in range(4):
                    dve.wait_ge(hn_hi_ready, 4 * t + b + 1)
                    dve.tensor_tensor(act_lo[:, 4 * b:4 * b + 4, t * P:(t + 1) * P],
                                      banks[:, (t % 2) * 4 + b, :].rearrange("p (k s) -> p k s", k=4),
                                      act_hi[:, 4 * b:4 * b + 4, t * P:(t + 1) * P], ALU.subtract
                                      ).then_inc(hn_lo_ready, 1)
            for q in range(3):
                split(q, q)
            dve.wait_ge(x_turned, 4 * ST)
            dve.wait_ge(x_squared, ST)
            dve.memset(u_buf[:, 0:2], 0.0).then_inc(u_zeroed, 1)
            for kv in range(KVH):
                dve.memset(logits[kv][:, :, 0:CHUNK], NEG).then_inc(neg_written, 1)
            dve.wait_ge(small_loaded, 16 * 7)
            for kv in range(KVH):
                for par in range(2):
                    rows = slice(par * CHUNK, (par + 1) * CHUNK)
                    sink = sink_row[rows, :].rearrange("p (v j a) -> p v j a", v=KVH, a=2)[:, kv, :, par]
                    dve.tensor_copy(logits[kv][rows, :, BAND], sink).then_inc(sinks_placed, 1)

            def stage_lo(tile, par):
                dve.wait_ge(hi_staged, tile + 1)
                dve.tensor_tensor(stage[:, 1, :].bitcast(F32R).rearrange("p (a s) -> p a s", a=2),
                                  proj[par], stage[:, 0, :].rearrange("p (a s) -> p a s", a=2), ALU.subtract
                                  ).then_inc(proj_free, 1)

            def silu(out_ap, count, par):
                dve.wait_ge(gate_exp, count)
                dve.tensor_scalar(h_buf, h_buf, 1.0, None, ALU.add).then_inc(gate_divisor, 1)
                dve.wait_ge(gate_divisor, count)
                dve.reciprocal(h_buf, h_buf).then_inc(sigmoid_ready, 1)
                dve.wait_ge(sigmoid_ready, count)
                dve.tensor_tensor(out_ap.rearrange("p (a s) -> p a s", a=2), proj[par],
                                  h_buf.rearrange("p (a s) -> p a s", a=2), ALU.mult).then_inc(proj_free, 1)

            def attn_gate(tile, par, first=False):
                if not first:
                    dve.wait_ge(gate_stored, (tile - QKV_TILES) * 16)
                silu(y_buf, tile - (QKV_TILES - 1), par)

            def splits(e, middle=None):
                split(e * 4 + 3, 3)
                if middle:
                    middle()
                for q in range(3):
                    split(e * 4 + 4 + q, q)

            splits(0)
            with dve.Fori(0, QKV_TILES // 2) as i:
                for par in range(2):
                    splits(i * 2 + (1 + par), lambda: stage_lo(i * 2 + par, par))

            def gate_pair(i, first):
                for par in range(2):
                    splits(i * 2 + (1 + par), lambda: attn_gate(i * 2 + par, par, first and par == 0))

            gate_pair(QKV_TILES // 2, True)
            with dve.Fori(QKV_TILES // 2 + 1, A_TILES // 2 - 1) as i:
                gate_pair(i, False)
            splits(A_TILES - 1, lambda: attn_gate(A_TILES - 2, 0))
            dve.wait_ge(bias_loaded, 32)

            def shift_logits(unit, kv, first_chunk):
                dve.wait_ge(qk_done, unit + 1)
                lo = CHUNK if first_chunk else 0
                dve.scalar_tensor_tensor(out=logits[kv][:, :, lo:BAND],
                                         in0=logit_ps.rearrange("p (j k) -> p j k", j=PAIRS)[:, :, lo:],
                                         scalar=SCALE, in1=bias[:, kv * PAIRS:(kv + 1) * PAIRS, lo:],
                                         op0=ALU.mult, op1=ALU.add).then_inc(logits_read, 1)
                dve.wait_ge(logits_read, unit + 1)
                if first_chunk:
                    dve.wait_ge(neg_written, KVH)
                    dve.wait_ge(sinks_placed, 2 * KVH)
                dve.tensor_reduce(row_max, logits[kv], AX_X, ALU.max).then_inc(max_ready, 1)
                dve.wait_ge(max_ready, unit + 1)
                if not (isinstance(unit, int) and unit == 0):
                    dve.wait_ge(probs_turned, unit)
                dve.tensor_tensor(probs, logits[kv], row_max.unsqueeze(2).to_broadcast([P, PAIRS, LW]),
                                  ALU.subtract).then_inc(shifted, 1)

            def normalise(unit):
                dve.wait_ge(exp_done, unit + 1)
                dve.tensor_reduce(row_sum, probs, AX_X, ALU.add).then_inc(sum_ready, 1)
                dve.wait_ge(sum_ready, unit + 1)
                dve.reciprocal(row_inv, row_sum).then_inc(inv_ready, 1)
                dve.wait_ge(inv_ready, unit + 1)
                dve.tensor_tensor(probs[:, :, 0:BAND], probs[:, :, 0:BAND],
                                  row_inv.unsqueeze(2).to_broadcast([P, PAIRS, BAND]), ALU.mult
                                  ).then_inc(probs_ready, 1)

            def gate_output(unit, first):
                dve.wait_ge(pv_done, unit + 1)
                dve.wait_ge(g_loaded, unit * 16 + 16)
                if not first:
                    dve.wait_ge(o_stored, unit * 16)
                o = o_ps.rearrange("p (j a k) -> p j a k", j=PAIRS, a=2)
                for par in range(2):
                    rows = slice(par * HEAD, (par + 1) * HEAD)
                    op = dve.tensor_tensor(o_mix[rows, :, :], o[rows, :, par, :], g_cur[rows, :, :], ALU.mult)
                op.then_inc(o_ready, 1)

            def halves(ap):
                return ap.rearrange("p (a s) -> p a s", a=2)

            def conv_h(g, e):
                dve.wait_ge(w_free, e * 4 + 8)
                dve.tensor_copy(halves(h_buf), proj[0]).then_inc(proj_free, 1)

            def conv_c(g, e, first):
                dve.wait_ge(w_free, e * 4 + 8)
                dve.wait_ge(proj_free, e + 2)
                dve.tensor_tensor(halves(u_buf[:, 2:]), proj[1], halves(h_buf), ALU.mult).then_inc(proj_free, 1)
                dve.wait_ge(proj_free, e + 3)
                if first:
                    dve.wait_ge(gate_stored, 16 * (A_TILES - QKV_TILES))
                    dve.wait_ge(u_zeroed, 1)
                else:
                    dve.wait_ge(conv_stored, g * 16)
                dve.tensor_scalar(y_buf, u_buf[:, 2:2 + S], tap_ap(2, g), tap_ap(3, g), ALU.mult, ALU.add
                                  ).then_inc(conv_step, 1)
                for t in (1, 0):
                    dve.wait_ge(conv_step, g * 3 + 2 - t)
                    dve.scalar_tensor_tensor(out=y_buf, in0=u_buf[:, t:t + S], scalar=tap_ap(t, g), in1=y_buf,
                                             op0=ALU.mult, op1=ALU.add).then_inc(conv_step, 1)

            def tap_ap(t, g):
                return taps[:, t, bass.ds(g, 1)]

            def conv_b_gate(g, e):
                dve.wait_ge(w_free, e * 4 + 8)
                dve.wait_ge(conv_step, g * 3 + 3)
                dve.tensor_tensor(halves(y_buf), proj[0], halves(y_buf), ALU.mult).then_inc(proj_free, 1)

            def conv_gate(g, e):
                dve.wait_ge(conv_step, g * 3 + 3)
                silu(u_buf[:, 2:], g + (A_TILES - QKV_TILES + 1), 1)
                dve.wait_ge(proj_free, e + 3)
                dve.tensor_tensor(y_buf, y_buf, u_buf[:, 2:], ALU.mult).then_inc(conv_out, 1)

            def mix_lo(t):
                dve.wait_ge(mix_hi_ready, t + 1)
                dve.tensor_tensor(act_lo[:, t, :], stage[:, t % 2, :], act_hi[:, t, :], ALU.subtract
                                  ).then_inc(mix_lo_ready, 1)

            def group(g, first, last):
                for kind in range(4):
                    e = g * 4 + A_TILES + kind
                    unit = g * 4 + kind
                    if not (first and kind == 0):
                        gate_output(unit - 1, first and kind == 1)
                    shift_logits(unit, kind % 2, first and kind < 2)
                    split(e * 4 + 3, 3)
                    normalise(unit)
                    split(e * 4 + 4, 0)
                    if kind == 0:
                        if first:
                            attn_gate(A_TILES - 1, 1)
                        else:
                            conv_gate(g - 1, e - 1)
                    elif kind == 1:
                        conv_h(g, e - 1)
                    elif kind == 2:
                        conv_c(g, e - 1, first)
                    else:
                        conv_b_gate(g, e - 1)
                    dve.wait_ge(pt_hi_ready, unit + 1)
                    dve.tensor_tensor(pt_lo[:, :], pt_ps, pt_hi[:, :], ALU.subtract).then_inc(pt_lo_ready, 1)
                    split(e * 4 + 5, 1)
                    if last and kind == 3:
                        mix_lo(0)
                    split(e * 4 + 6, 2)
                    if last and kind == 3:
                        mix_lo(1)

            group(0, True, False)
            with dve.Fori(1, GROUPS - 1) as g:
                group(g, False, False)
            group(GROUPS - 1, False, True)

            mix_lo(2)
            gate_output(UNITS - 1, False)
            conv_gate(GROUPS - 1, TILES - 1)
            mix_lo(3)

            def add_resid(r):
                b, st = r // 4, r % 4
                if st < 3:
                    dve.wait_ge(out_done, 3 * b + st + 1)
                else:
                    dve.wait_ge(w_free, WO_Q + 4 + (b + 1) * KT)
                dve.wait_ge(resid_loaded[r % 2], 16 * (r // 2 + 1))
                if r == 0:
                    dve.wait_ge(conv_stored, 16 * GROUPS)
                    dve.wait_ge(o_stored, 16 * UNITS)
                if r == 16:
                    dve.wait_ge(out_stored, 16 * 4)
                dve.tensor_tensor(y_res[:, st, (b % 4) * N:(b % 4 + 1) * N], banks[:, 4 - 4 * (b % 2) + st, :],
                                  resid[:, r % 2, :], ALU.add).then_inc(y_ready, 1)

            def final_rstd(half):
                dve.wait_ge(bank_free, 8 + 16 * (half + 1))
                dve.tensor_reduce(y_ssq, ssq[:, :, :], AX_X, ALU.add).then_inc(y_ssq_ready, 1)
                dve.wait_ge(y_ssq_ready, half + 1)
                dve.tensor_scalar(y_var, y_ssq, 1.0 / D, EPS, ALU.mult, ALU.add).then_inc(y_var_ready, 1)
                dve.wait_ge(y_rstd_ready, half + 1)

            def finish(st, c):
                cols = slice(c * N, (c + 1) * N)
                dve.scalar_tensor_tensor(out=y_res[:, st, cols], in0=y_res[:, st, cols],
                                         scalar=y_rstd[:, st:st + 1], in1=final_row[:, cols],
                                         op0=ALU.mult, op1=ALU.mult).then_inc(y_final, 1)

            for b in range(BLOCKS):
                for k in range(KT):
                    piece = b * KT + k + 3
                    if piece < BLOCKS * KT:
                        split(WO_Q + piece, piece % 4)
                    if b == 0 and k + 4 < KT:
                        mix_lo(k + 4)
                    if b > 0 and k < 4:
                        add_resid(4 * (b - 1) + k)
                    if b == 4:
                        if k == 4:
                            dve.wait_ge(final_row_loaded, 16)
                            final_rstd(0)
                        if 4 <= k < 12:
                            finish((k - 4) // 2, (k - 4) % 2 * 2)
                            finish((k - 4) // 2, (k - 4) % 2 * 2 + 1)
            for st in range(4):
                add_resid(4 * (BLOCKS - 1) + st)
            final_rstd(1)
            for st in range(4):
                for c in range(4):
                    finish(st, c)

        @block.tensor
        def _(pe):
            pe.wait_ge(ident_ready, 1)
            pe.wait_ge(small_loaded, 16 * 7)
            rows = (TAPS + 1) * GROUPS
            pe.transpose(banks[:, 7, 0:rows], tap_rows, ident[0:rows, 0:rows]).then_inc(taps_turned, 1)
            pe.matmul(banks[0:HEADS, 6, 0:REL], rel_rows, hot_rows, start=True, stop=True
                      ).then_inc(taps_turned, 1)

            for t in range(ST):
                pe.wait_ge(x_normed, t + 1)
                for b in range(4):
                    bank = (t % 2) * 4 + b
                    if t >= 2:
                        pe.wait_ge(hn_lo_ready, 4 * (t - 2) + b + 1)
                    elif t == 1 and b == 2:
                        pe.wait_ge(rel_copied, 1)
                        pe.wait_ge(rel_looked_up, 1)
                    for j in range(4):
                        k = 4 * b + j
                        op = pe.transpose(banks[:, bank, j * P:(j + 1) * P], x_tile[t % 2][:, k * P:(k + 1) * P],
                                          ident[:, :])
                    op.then_inc(x_turned, 1)

            def quarter(q, count, par):
                pe.wait_ge(w_lo_ready, count + 1)
                for j in range(QK):
                    k = q * QK + j
                    wh = w_hi[:, q, j * P:(j + 1) * P]
                    wl = w_lo[:, q, j * P:(j + 1) * P]
                    for w, a, s in ((wh, act_hi, 0), (wh, act_hi, 1), (wh, act_lo, 0), (wh, act_lo, 1),
                                    (wl, act_hi, 0), (wl, act_hi, 1)):
                        op = pe.matmul(proj[par][:, s, :], w, a[:, k, s * N:(s + 1) * N],
                                       start=(k == 0 and w is wh and a is act_hi),
                                       stop=(k == KT - 1 and w is wl))
                return op

            pe.wait_ge(hn_lo_ready, 4 * ST)
            with pe.Fori(0, A_TILES // 2) as i:
                for par in range(2):
                    pe.wait_ge(proj_free, i * 2 + (par + 1))
                    for q in range(4):
                        quarter(q, i * 8 + (4 * par + q), par).then_inc(w_free, 1)

            with pe.Fori(0, GROUPS) as g:
                for kind in range(4):
                    e = g * 4 + (A_TILES + kind)
                    unit = g * 4 + kind
                    kv = kind % 2
                    pe.wait_ge(qk_loaded, unit * 64 + 64)
                    for j in range(PAIRS):
                        for c in range(2):
                            op = pe.matmul(logit_ps[:, j * BAND:(j + 1) * BAND],
                                           q_cur[:, 2 * j:2 * j + 2, :].rearrange("p h s -> p (h s)"),
                                           k_cur[:, c, :], start=(c == 0), stop=(c == 1))
                    op.then_inc(qk_done, 1)
                    pe.wait_ge(proj_free, e + 1)
                    quarter(0, e * 4, kind % 2).then_inc(w_free, 1)
                    if kv == 0:
                        pe.wait_ge(v_loaded, (g * 2 + kind // 2) * 16 + 16)
                        for c in range(2):
                            op = pe.transpose(v_ps[:, c * P:(c + 1) * P], v_win[:, c, :], ident[:, :])
                        op.then_inc(v_turned, 1)
                    quarter(1, e * 4 + 1, kind % 2).then_inc(w_free, 1)
                    pe.wait_ge(probs_ready, unit + 1)
                    for j in range(PAIRS):
                        op = pe.transpose(pt_ps[:, j * P:(j + 1) * P], probs[:, j, 0:BAND], ident[:, :])
                    op.then_inc(probs_turned, 1)
                    quarter(2, e * 4 + 2, kind % 2).then_inc(w_free, 1)
                    quarter(3, e * 4 + 3, kind % 2).then_inc(w_free, 1)
                    pe.wait_ge(pt_lo_ready, unit + 1)
                    pe.wait_ge(v_ready, g * 2 + (kind // 2 + 1))
                    vh, vl = (v_cur[:, c, kv, :, :].rearrange("p a d -> p (a d)") for c in range(2))
                    for i, (v, pt) in enumerate(((vh, pt_hi), (vh, pt_lo), (vl, pt_hi))):
                        op = pe.matmul(o_ps, v, pt[:, :], start=(i == 0), stop=(i == 2))
                    op.then_inc(pv_done, 1)

            def out_block(b, par, half, first):
                for k in range(KT):
                    pe.wait_ge(w_lo_ready, b * KT + (WO_Q + k + 1))
                    if first:
                        pe.wait_ge(mix_lo_ready, k + 1)
                    for st in range(4):
                        tok = slice(half * N + st * P, half * N + (st + 1) * P)
                        if k == 0:
                            pe.wait_ge(bank_free, b * 4 + (st + 1))
                            if first and par == 0 and st == 0:
                                pe.wait_ge(v_ready, NC)
                            if first and par == 0 and st == 3:
                                pe.wait_ge(o_ready, UNITS)
                            if first and par == 1 and st == 0:
                                pe.wait_ge(proj_free, TILES + 2)
                        bank = banks[:, 4 - 4 * par + st, :]
                        for i, (a, w) in enumerate(((act_hi, w_hi), (act_hi, w_lo), (act_lo, w_hi))):
                            op = pe.matmul(bank, a[:, k, tok], w[:, k % 4, :], start=(k == 0 and i == 0),
                                           stop=(k == KT - 1 and i == 2))
                        if k == KT - 1 and st < 3:
                            op.then_inc(out_done, 1)
                    op.then_inc(w_free, 1)

            for half in range(SH):
                with pe.Fori(half * 2, half * 2 + 2) as i:
                    for par in range(2):
                        out_block(i * 2 + par, par, half, half == 0)


_INS = ["x", "norm_w", "w_in", "sinks", "conv_w", "conv_b", "w_out", "rel_bias", "final_norm_w"]


def kernel(**inputs):
    import numpy as _np
    import concourse.bacc as _bacc
    from concourse import mybir as _mybir
    from concourse.bass_utils import run_bass_kernel_spmd as _run

    nc = _bacc.Bacc("TRN2", target_bir_lowering=False, num_devices=1)
    given = {name: _np.ascontiguousarray(inputs[name]) for name in _INS}
    given["one_hot"] = t5_one_hot()
    arrays, args = {}, []
    for name, a in given.items():
        arrays[f"in_{name}_dram"] = a
        args.append(nc.dram_tensor(f"in_{name}_dram", a.shape, _mybir.dt.from_np(a.dtype), kind="ExternalInput").ap())
    args.append(nc.dram_tensor("out_0_dram", (1, S, D), F32, kind="ExternalOutput").ap())
    build(nc, *args)
    r = _run(nc, [arrays], core_ids=[0])
    return r.results[0]["out_0_dram"]
```

```python
import math
from contextlib import ExitStack

import numpy as np
import concourse.bass as bass
from concourse import mybir

F32 = mybir.dt.float32
F32R = mybir.dt.float32r
ALU = mybir.AluOpType
ACT = mybir.ActivationFunctionType
AX_X = mybir.AxisListType.X

P = 128
D = 2048
S = 1024
CHUNK = 64
HEAD = 64
BAND = 2 * CHUNK
HEADS = 16
KVH = 2
PAIRS = HEADS // KVH // 2
ATTN = HEADS * HEAD
CONV = 1024
TAPS = 3
IN_COLS = 2 * ATTN + 2 * KVH * HEAD + 4 * CONV
BUCKETS = 32
MAX_DISTANCE = 128
EPS = 1e-6
NEG = -1e30
SCALE = 1.0 / math.sqrt(HEAD)

KT = D // P
QK = KT // 4
ST = S // P
NC = S // CHUNK
N = 512
SH = S // N
QKV_TILES = (ATTN + 2 * KVH * HEAD) // P
K_ROW = ATTN
V_ROW = ATTN + KVH * HEAD
A_TILES = QKV_TILES + ATTN // P
GROUPS = CONV // P
TILES = A_TILES + 4 * GROUPS
UNITS = NC * KVH
REL = 192
XR = 3
MR = 4
BLOCKS = SH * (D // N)
WO_Q = 4 * TILES


def t5_one_hot():
    rel = np.arange(REL) - (BAND - 1)
    n = -rel
    half = BUCKETS // 2
    ret = (n < 0).astype(np.int32) * half
    n = np.abs(n)
    max_exact = half // 2
    nf = np.maximum(n, 1).astype(np.float32)
    large = max_exact + (np.log(nf / max_exact) / math.log(MAX_DISTANCE / max_exact)
                         * (half - max_exact)).astype(np.int32)
    large = np.minimum(large, half - 1)
    bucket = ret + np.where(n < max_exact, n, large).astype(np.int32)
    return (bucket[None, :] == np.arange(BUCKETS)[:, None]).astype(np.float32)


def build(nc, x, norm_w, w_in, sinks, conv_w, conv_b, w_out, rel_bias, final_norm_w, one_hot, out):
    ctx = ExitStack()
    with ctx:
        def sb(name, shape, dt=F32):
            return ctx.enter_context(nc.sbuf_tensor(name, shape, dt))

        def sem(name):
            return ctx.enter_context(nc.semaphore(name))

        qkv_park = nc.dram_tensor("qkv_park", [2, QKV_TILES * P, CHUNK + S], F32, kind="Internal").ap()
        gate_park = nc.dram_tensor("gate_park", [ATTN, S], F32, kind="Internal").ap()
        mix_park = nc.dram_tensor("mix_park", [ATTN + CONV, S], F32, kind="Internal").ap()
        rel_park = nc.dram_tensor("rel_park", [HEADS, CHUNK, REL], F32, kind="Internal").ap()

        act_hi = sb("act_hi", [P, KT, S], F32R)
        act_lo = sb("act_lo", [P, KT, S], F32R)
        w_raw = sb("w_raw", [P, 4, N])
        w_hi = sb("w_hi", [P, 4, N], F32R)
        w_lo = sb("w_lo", [P, 4, N], F32R)
        q_cur = sb("q_cur", [P, PAIRS * 2, CHUNK], F32R)
        k_cur = sb("k_cur", [P, 2, BAND], F32R)
        pt_hi = sb("pt_hi", [P, N], F32R)
        pt_lo = sb("pt_lo", [P, N], F32R)
        v_cur = sb("v_cur", [P, 2, KVH, 2, HEAD], F32R)
        ident = sb("ident", [P, P])
        taps = sb("taps", [P, TAPS + 1, GROUPS])
        small = sb("small", [P, 68])
        ssq = sb("ssq", [P, 4, 4])

        arena = sb("arena", [P, 4 * D])
        stage = sb("stage", [P, 2, S])
        resid = sb("resid", [P, 2, N])

        off = [0]

        def carve(n):
            off[0] += n
            return arena[:, off[0] - n:off[0]]

        h_buf = carve(S)
        u_buf = carve(2 + S)
        y_buf = carve(S)
        bias = carve(HEADS // 2 * BAND).rearrange("p (j k) -> p j k", j=HEADS // 2)
        LW = BAND + 1
        logits = [carve(PAIRS * LW).rearrange("p (j k) -> p j k", j=PAIRS) for _ in range(KVH)]
        probs = carve(PAIRS * LW).rearrange("p (j k) -> p j k", j=PAIRS)
        v_win = carve(2 * BAND).rearrange("p (c k) -> p c k", c=2)
        g_cur = carve(PAIRS * CHUNK).rearrange("p (j k) -> p j k", j=PAIRS)
        o_mix = carve(PAIRS * CHUNK).rearrange("p (j k) -> p j k", j=PAIRS)
        assert off[0] <= 4 * D
        x_tile = [arena[:, i * D:(i + 1) * D] for i in range(XR)]
        norm_row = arena[:, 3 * D:4 * D]
        square = stage[:, :, :].rearrange("p a s -> p (a s)")
        setup = resid[:, :, :].rearrange("p a s -> p (a s)")
        tap_rows = setup[0:(TAPS + 1) * GROUPS, 0:P]
        rel_rows = setup[0:BUCKETS, P:P + HEADS]
        hot_rows = setup[0:BUCKETS, 256:256 + REL]
        rel_tab = setup[0:HEADS, 512:512 + REL]
        zeros = setup[:, 768:768 + CHUNK]
        mix_raw = [stage[:, 0, :], stage[:, 1, :], setup, carve(S)]
        assert off[0] <= 4 * D
        y_res = arena[:, :].rearrange("p (t c) -> p t c", t=4)
        final_row = stage[:, :, :].rearrange("p a s -> p (a s)")

        row_max = small[:, 0:4]
        row_sum = small[:, 4:8]
        row_inv = small[:, 8:12]
        minus_half = small[:, 64:68]
        x_ssq = small[:, 12:20]
        x_var = small[:, 20:28]
        x_rstd = small[:, 28:36]
        y_ssq = small[:, 36:40]
        y_var = small[:, 40:44]
        y_rstd = small[:, 44:48]
        sink_row = small[:, 48:64]

        banks = ctx.enter_context(nc.psum_tensor("banks", [P, 8, N], F32))
        proj = [banks[:, 0:2, :], banks[:, 2:4, :]]
        v_ps, logit_ps, pt_ps, o_ps = (banks[:, b, :] for b in range(4, 8))

        ident_zero = sem("ident_zero")
        minus_half_ready = sem("minus_half_ready")
        ident_ready = sem("ident_ready")
        small_loaded = sem("small_loaded")
        u_zeroed = sem("u_zeroed")
        zeros_ready = sem("zeros_ready")
        pad_stored = sem("pad_stored")
        taps_turned = sem("taps_turned")
        taps_copied = sem("taps_copied")
        rel_copied = sem("rel_copied")
        rel_stored = sem("rel_stored")
        bias_loaded = sem("bias_loaded")
        neg_written = sem("neg_written")
        sinks_placed = sem("sinks_placed")
        norm_row_loaded = sem("norm_row_loaded")
        x_loaded = [sem(f"x_loaded{i}") for i in range(XR)]
        x_weighted = sem("x_weighted")
        x_squared = sem("x_squared")
        x_var_ready = sem("x_var_ready")
        x_rstd_ready = sem("x_rstd_ready")
        x_normed = sem("x_normed")
        x_turned = sem("x_turned")
        hn_hi_ready = sem("hn_hi_ready")
        hn_lo_ready = sem("hn_lo_ready")
        raw_loaded = [sem(f"raw_loaded{i}") for i in range(4)]
        w_hi_ready = sem("w_hi_ready")
        w_lo_ready = sem("w_lo_ready")
        w_free = sem("w_free")
        proj_free = sem("proj_free")
        hi_staged = sem("hi_staged")
        qkv_stored = sem("qkv_stored")
        gate_exp = sem("gate_exp")
        gate_divisor = sem("gate_divisor")
        sigmoid_ready = sem("sigmoid_ready")
        gate_stored = sem("gate_stored")
        conv_step = sem("conv_step")
        conv_stored = sem("conv_stored")
        qk_loaded = sem("qk_loaded")
        v_loaded = sem("v_loaded")
        g_loaded = sem("g_loaded")
        qk_done = sem("qk_done")
        logits_read = sem("logits_read")
        max_ready = sem("max_ready")
        shifted = sem("shifted")
        exp_done = sem("exp_done")
        sum_ready = sem("sum_ready")
        inv_ready = sem("inv_ready")
        probs_ready = sem("probs_ready")
        probs_turned = sem("probs_turned")
        pt_hi_ready = sem("pt_hi_ready")
        pt_lo_ready = sem("pt_lo_ready")
        v_turned = sem("v_turned")
        v_ready = sem("v_ready")
        pv_done = sem("pv_done")
        o_ready = sem("o_ready")
        o_stored = sem("o_stored")
        mix_loaded = [sem(f"mix_loaded{i}") for i in range(MR)]
        mix_hi_ready = sem("mix_hi_ready")
        mix_lo_ready = sem("mix_lo_ready")
        out_done = sem("out_done")
        bank_free = sem("bank_free")
        resid_loaded = [sem(f"resid_loaded{i}") for i in range(2)]
        y_ready = sem("y_ready")
        y_ssq_ready = sem("y_ssq_ready")
        y_var_ready = sem("y_var_ready")
        y_rstd_ready = sem("y_rstd_ready")
        final_row_loaded = sem("final_row_loaded")
        y_final = sem("y_final")
        y_weighted = sem("y_weighted")
        y_last_final = sem("y_last_final")
        y_final_act = sem("y_final_act")
        out_stored = sem("out_stored")
        out_stored_last = sem("out_stored_last")

        w_in_v = w_in[0].rearrange("(k p) c -> p k c", p=P)
        w_out_v = w_out[0].rearrange("(k p) c -> p k c", p=P)
        x_v = x[0].rearrange("(t p) d -> p t d", p=P)
        out_v = out[0].rearrange("(t p) d -> p t d", p=P)
        qkv_v = qkv_park.rearrange("c (m p) s -> p c m s", p=P)
        qkv_head = qkv_park.rearrange("c (h d) s -> d c h s", d=HEAD)
        gate_v = gate_park.rearrange("(m p) s -> p m s", p=P)
        mix_v = mix_park.rearrange("(m p) s -> p m s", p=P)

        def mix_row_tile(t):
            return (t + ATTN // P) % KT

        def conv_col(kind, g):
            return A_TILES * P + (0, 1, 3, 2)[kind] * CONV + g * P

        def turn_bank(t, b):
            return (t % 2 if t < 4 else 1) * 4 + b

        block = ctx.enter_context(nc.Block())

        @block.sync
        def _(sp):
            def at(column):
                return column if isinstance(column, int) else sp.snap(column)

            def load_in(slot, quarter, col):
                col = at(col)
                if not (isinstance(quarter, int) and quarter < 4):
                    sp.wait_ge(w_lo_ready, quarter - 3)
                sp.dma_start(w_raw[:, slot, :].rearrange("p (k c) -> p k c", k=QK),
                             w_in_v[:, slot * QK:(slot + 1) * QK, bass.ds(col, P)]
                             ).then_inc(raw_loaded[slot], 16)

            def load_out(slot, piece, row_tile, dblk):
                sp.wait_ge(w_lo_ready, WO_Q + piece - 3)
                sp.dma_start(w_raw[:, slot, :], w_out_v[:, row_tile, dblk * N:(dblk + 1) * N]
                             ).then_inc(raw_loaded[slot], 16)

            def load_qk(queries, band, kv):
                for c in range(2):
                    half = slice(c * HEAD, (c + 1) * HEAD)
                    sp.dma_start(q_cur[half, :, :].bitcast(F32),
                                 qkv_head[:, c, kv * PAIRS * 2:(kv + 1) * PAIRS * 2,
                                          bass.ds(queries, CHUNK)]).then_inc(qk_loaded, 16)
                    sp.dma_start(k_cur[half, :, :].bitcast(F32),
                                 qkv_head[:, :, K_ROW // HEAD + kv, bass.ds(band, BAND)]
                                 ).then_inc(qk_loaded, 16)

            def load_v(band):
                sp.dma_start(v_win, qkv_v[:, :, V_ROW // P, bass.ds(band, BAND)]).then_inc(v_loaded, 16)

            def load_mix(t):
                if t >= MR:
                    sp.wait_ge(mix_lo_ready, t - MR + 1)
                if t < GROUPS:
                    sp.wait_ge(conv_stored, 16 * (t + 1))
                else:
                    sp.wait_ge(o_stored, 16 * UNITS)
                sp.dma_start(mix_raw[t % MR], mix_v[:, mix_row_tile(t), :]).then_inc(mix_loaded[t % MR], 16)

            sp.dma_start(x_tile[0], x_v[:, 0, :]).then_inc(x_loaded[0], 16)
            sp.dma_start(norm_row, bass.AP(tensor=norm_w.tensor, offset=0, ap=[[0, P], [1, D]])
                         ).then_inc(norm_row_loaded, 16)
            for t in range(1, XR):
                sp.dma_start(x_tile[t], x_v[:, t, :]).then_inc(x_loaded[t], 16)
            for q in range(4):
                load_in(q, q, 0)
            for t in range(XR, ST):
                sp.wait_ge(x_turned, 4 * (t - XR + 1))
                sp.dma_start(x_tile[t % XR], x_v[:, t, :]).then_inc(x_loaded[t % XR], 16)
                if t == XR:
                    for i in range(TAPS):
                        sp.dma_start(tap_rows[i * GROUPS:(i + 1) * GROUPS, :],
                                     conv_w[0, i].rearrange("(g p) -> g p", p=P)).then_inc(small_loaded, 16)
                    sp.dma_start(tap_rows[TAPS * GROUPS:, :],
                                 conv_b[0].rearrange("(g p) -> g p", p=P)).then_inc(small_loaded, 16)
                    sp.dma_start(rel_rows, rel_bias).then_inc(small_loaded, 16)
                    sp.dma_start(hot_rows, one_hot).then_inc(small_loaded, 16)
                    sp.dma_start(sink_row, bass.AP(tensor=sinks.tensor, offset=0, ap=[[0, P], [1, HEADS]])
                                 ).then_inc(small_loaded, 16)
            for q in range(3):
                load_in(q, 4 + q, P)
            sp.wait_ge(rel_stored, 16)
            sp.wait_ge(hn_lo_ready, 4 * ST)
            for par in range(2):
                sp.dma_start(bias[par * CHUNK:(par + 1) * CHUNK, :, :],
                             bass.AP(tensor=rel_park.tensor, offset=par * CHUNK * REL + CHUNK - 1,
                                     ap=[[REL - 1, CHUNK], [2 * CHUNK * REL, HEADS // 2], [1, BAND]])
                             ).then_inc(bias_loaded, 16)

            with sp.Fori(0, A_TILES - 1) as e:
                load_in(3, e * 4 + 7, e * P + P)
                for q in range(3):
                    load_in(q, e * 4 + 8 + q, e * P + 2 * P)
            e = A_TILES - 1
            load_in(3, 4 * e + 7, conv_col(0, 0))
            for q in range(3):
                load_in(q, 4 * e + 8 + q, conv_col(1, 0))
            sp.wait_ge(qkv_stored, 32 * QKV_TILES)
            sp.wait_ge(pad_stored, 64)
            load_qk(CHUNK, 0, 0)
            load_v(0)
            def group(g, last):
                for kind in range(4):
                    e = g * 4 + A_TILES + kind
                    unit = g * 4 + kind
                    if not (last and kind == 3):
                        band = at((g * 2 + (kind + 1) // 2) * CHUNK)
                        queries = at((g * 2 + (kind + 1) // 2) * CHUNK + CHUNK)
                        sp.wait_ge(qk_done, unit + 1)
                        load_qk(queries, band, (kind + 1) % 2)

                    def raw(k):
                        ahead = kind + (1 if k == 0 else 2)
                        slot = (3 + k) % 4
                        if last and ahead >= 4:
                            piece = 4 * (ahead - 4) + slot
                            load_out(slot, piece, mix_row_tile(piece), 0)
                        else:
                            load_in(slot, e * 4 + 7 + k, conv_col(ahead % 4, g + ahead // 4))

                    raw(0)
                    raw(1)
                    if kind % 2 == 0 and not (last and kind == 2):
                        band = at((g * 2 + kind // 2 + 1) * CHUNK)
                        sp.wait_ge(v_turned, g * 2 + kind // 2 + 1)
                        load_v(band)
                    if last and kind == 3:
                        for t in range(MR):
                            load_mix(t)
                    raw(2)
                    raw(3)

            group(0, False)
            with sp.Fori(1, GROUPS - 1) as g:
                group(g, False)
            group(GROUPS - 1, True)

            def load_resid(r):
                half, dblk, st = r // 16, r // 4 % 4, r % 4
                if r >= 2:
                    sp.wait_ge(y_ready, r - 1)
                sp.dma_start(resid[:, r % 2, :], x_v[:, half * 4 + st, dblk * N:(dblk + 1) * N]
                             ).then_inc(resid_loaded[r % 2], 16)

            for b in range(BLOCKS):
                for k in range(KT):
                    piece = b * KT + k
                    ahead = piece + 7
                    if b > 0 and k in (2, 3):
                        load_resid(4 * b - 4 + k)
                    if ahead < BLOCKS * KT:
                        load_out(ahead % 4, ahead, mix_row_tile(ahead % KT), ahead // KT % 4)
                    if b == 0 and k + MR < KT:
                        load_mix(k + MR)
                    if k == KT - 2:
                        if b == 0:
                            sp.wait_ge(mix_lo_ready, KT - 1)
                            sp.dma_start(final_row, bass.AP(tensor=final_norm_w.tensor, offset=0,
                                                            ap=[[0, P], [1, D]])).then_inc(final_row_loaded, 16)
                        load_resid(4 * b)
                        load_resid(4 * b + 1)
            load_resid(4 * BLOCKS - 2)
            load_resid(4 * BLOCKS - 1)
            for st in range(4):
                sp.wait_ge(y_last_final, st + 1)
                if st < 2:
                    sp.wait_ge(y_final, 4 + st + 1)
                else:
                    sp.wait_ge(y_final_act, st - 1)
                sp.dma_start(out_v[:, 4 + st, :], y_res[:, st, :]).then_inc(out_stored_last, 16)
            sp.wait_ge(out_stored, 16 * 4)
            sp.wait_ge(out_stored_last, 16 * 4)

        @block.gpsimd
        def _(pool):
            pool.sem_inc(w_free, 4)
            pool.sem_inc(proj_free, 2)
            pool.sem_inc(bank_free, 8)
            pool.memset(ident[:, :], 0.0).then_inc(ident_zero, 1)
            pool.memset(minus_half, -0.5).then_inc(minus_half_ready, 1)
            pool.wait_ge(ident_zero, 1)
            pool.affine_select(out=ident[:, :], in_=ident[:, :], compare_op=ALU.not_equal, fill=1.0, base=0,
                               pattern=[[-1, P]], channel_multiplier=1).then_inc(ident_ready, 1)
            pool.wait_ge(minus_half_ready, 1)
            pool.wait_ge(norm_row_loaded, 16)
            for t in range(ST):
                pool.wait_ge(x_squared, t + 1)
                pool.tensor_tensor(x_tile[t % XR], x_tile[t % XR], norm_row, ALU.mult).then_inc(x_weighted, 1)
                pool.wait_ge(x_var_ready, t + 1)
                pool.tensor_tensor(x_rstd[:, t:t + 1], x_var[:, t:t + 1], minus_half[:, 0:1], ALU.pow
                                   ).then_inc(x_rstd_ready, 1)
            pool.wait_ge(zeros_ready, 1)
            for c in range(2):
                for m in (K_ROW // P, V_ROW // P):
                    pool.dma_start(qkv_v[:, c, m, 0:CHUNK], zeros).then_inc(pad_stored, 16)
            pool.wait_ge(rel_copied, 1)
            pool.dma_start(rel_park, rel_tab.unsqueeze(1).to_broadcast([HEADS, CHUNK, REL])).then_inc(rel_stored, 16)

            with pool.Fori(0, QKV_TILES) as m:
                pool.wait_ge(proj_free, m + 3)
                for c in range(2):
                    pool.dma_start(qkv_v[:, c, bass.ds(m, 1), CHUNK:].rearrange("p a s -> p (a s)"),
                                   stage[:, c, :]).then_inc(qkv_stored, 16)
            with pool.Fori(0, A_TILES - QKV_TILES) as m:
                pool.wait_ge(proj_free, m + (QKV_TILES + 3))
                pool.dma_start(gate_v[:, bass.ds(m, 1), :].rearrange("p a s -> p (a s)"), y_buf
                               ).then_inc(gate_stored, 16)
            with pool.Fori(0, GROUPS) as g:
                for kind in range(4):
                    pool.wait_ge(o_ready, g * 4 + kind + 1)
                    pool.dma_start(mix_v[:, (kind % 2) * PAIRS:(kind % 2 + 1) * PAIRS,
                                         bass.ds((g * 2 + kind // 2) * CHUNK, CHUNK)], o_mix
                                   ).then_inc(o_stored, 16)
                pool.wait_ge(proj_free, g * 4 + (A_TILES + 6))
                pool.dma_start(mix_v[:, bass.ds(g + ATTN // P, 1), :].rearrange("p a s -> p (a s)"), y_buf
                               ).then_inc(conv_stored, 16)
            def weight_y(r):
                b, st = r // 4, r % 4
                cols = slice((b % 4) * N, (b % 4 + 1) * N)
                pool.wait_ge(bank_free, 8 + r + 1)
                pool.tensor_tensor(y_res[:, st, cols], y_res[:, st, cols], final_row[:, cols], ALU.mult
                                   ).then_inc(y_weighted, 1)

            def final_rstd(half):
                pool.wait_ge(y_var_ready, half + 1)
                pool.tensor_tensor(y_rstd, y_var, minus_half, ALU.pow).then_inc(y_rstd_ready, 1)

            pool.wait_ge(final_row_loaded, 16)
            for r in range(16):
                weight_y(r)
            final_rstd(0)
            for st in range(4):
                pool.wait_ge(y_final, st + 1)
                pool.dma_start(out_v[:, st, :], y_res[:, st, :]).then_inc(out_stored, 16)
            for r in range(16, 28):
                weight_y(r)
            final_rstd(1)

        @block.scalar
        def _(act):
            def split(slot, quarter, turn):
                act.wait_ge(raw_loaded[slot], turn * 16 + 16)
                act.wait_ge(w_free, quarter + 1)
                act.activation(w_hi[:, slot, :], w_raw[:, slot, :], ACT.Copy).then_inc(w_hi_ready, 1)

            def square_x(t):
                act.wait_ge(x_loaded[t % XR], 16 * (t // XR + 1))
                if t >= 1:
                    act.wait_ge(x_squared, t)
                act.activation(square, x_tile[t % XR], ACT.Square, accum_out=x_ssq[:, t:t + 1]
                               ).then_inc(x_squared, 1)

            square_x(0)
            for t in range(ST):
                if t + 1 < ST:
                    square_x(t + 1)
                for b in range(4):
                    act.wait_ge(x_turned, 4 * t + b + 1)
                    act.activation(act_hi[:, 4 * b:4 * b + 4, t * P:(t + 1) * P],
                                   banks[:, turn_bank(t, b), :].rearrange("p (k s) -> p k s", k=4), ACT.Copy
                                   ).then_inc(hn_hi_ready, 1)
                if 0 <= t <= 3:
                    split(t, t, 0)

            def stage_hi(e, par, first):
                act.wait_ge(w_free, e * 4 + 8)
                if not first:
                    act.wait_ge(qkv_stored, e * 32)
                act.activation(stage[:, 0, :].bitcast(F32R).rearrange("p (a s) -> p a s", a=2),
                               proj[par], ACT.Copy).then_inc(hi_staged, 1)

            def exp_gate(tile, par):
                act.wait_ge(w_free, tile * 4 + 8)
                act.wait_ge(proj_free, tile + 2)
                act.activation(h_buf.rearrange("p (a s) -> p a s", a=2), proj[par], ACT.Exp, scale=-1.0
                               ).then_inc(gate_exp, 1)

            def splits(e, middle=None):
                split(3, e * 4 + 3, e)
                if middle:
                    middle()
                for q in range(3):
                    split(q, e * 4 + 4 + q, e + 1)

            def qkv_pair(i, first):
                for par in range(2):
                    splits(i * 2 + (1 + par), lambda: stage_hi(i * 2 + par, par, first and par == 0))

            for q in range(3):
                split(q, 4 + q, 1)
            qkv_pair(0, True)
            with act.Fori(1, QKV_TILES // 2) as i:
                qkv_pair(i, False)
            with act.Fori(QKV_TILES // 2, A_TILES // 2 - 1) as i:
                for par in range(2):
                    splits(i * 2 + (1 + par), lambda: exp_gate(i * 2 + par, par))
            splits(A_TILES - 1, lambda: exp_gate(A_TILES - 2, 0))

            def group(g, last):
                for kind in range(4):
                    e = g * 4 + A_TILES + kind
                    unit = g * 4 + kind
                    act.wait_ge(shifted, unit + 1)
                    act.activation(probs, probs, ACT.Exp).then_inc(exp_done, 1)
                    split(3, e * 4 + 3, e)
                    if kind == 3:
                        exp_gate(e - 1, 0)
                    elif isinstance(g, int) and g == 0 and kind == 0:
                        exp_gate(e - 1, 1)
                    split(0, e * 4 + 4, e + 1)
                    if kind % 2 == 0:
                        n = g * 2 + kind // 2
                        act.wait_ge(v_turned, n + 1)
                        for c in range(2):
                            v_in = v_ps[:, c * P:(c + 1) * P].rearrange("p (h d) -> p h d", h=KVH)
                            for copy in range(2):
                                op = act.activation(v_cur[:, c, :, copy, :], v_in, ACT.Copy)
                        op.then_inc(v_ready, 1)
                    act.wait_ge(probs_turned, unit + 1)
                    act.activation(pt_hi[:, :], pt_ps, ACT.Copy).then_inc(pt_hi_ready, 1)
                    if isinstance(g, int) and g == 0 and kind == 0:
                        act.wait_ge(gate_stored, 16 * (A_TILES - QKV_TILES))
                    act.dma_start(g_cur, gate_v[:, (kind % 2) * PAIRS:(kind % 2 + 1) * PAIRS,
                                                bass.ds((g * 2 + kind // 2) * CHUNK, CHUNK)]
                                  ).then_inc(g_loaded, 16)
                    split(1, e * 4 + 5, e + 1)
                    if last and kind == 3:
                        mix_hi(0)
                    split(2, e * 4 + 6, e + 1)
                    if last and kind == 3:
                        for t in range(1, MR):
                            mix_hi(t)

            def mix_hi(t):
                act.wait_ge(mix_loaded[t % MR], 16 * (t // MR + 1))
                act.wait_ge(w_free, 4 * TILES + t // 4 + 1)
                act.activation(act_hi[:, t, :], mix_raw[t % MR], ACT.Copy).then_inc(mix_hi_ready, 1)

            group(0, False)
            with act.Fori(1, GROUPS - 1) as g:
                group(g, False)
            group(GROUPS - 1, True)

            def square_y(r):
                act.wait_ge(y_ready, r + 1)
                b, st = r // 4, r % 4
                act.activation(banks[:, 4 - 4 * (b % 2) + st, :], y_res[:, st, (b % 4) * N:(b % 4 + 1) * N],
                               ACT.Square, accum_out=ssq[:, st, b % 4:b % 4 + 1]).then_inc(bank_free, 1)

            for b in range(BLOCKS):
                for k in range(KT):
                    piece = b * KT + k + 3
                    if piece < BLOCKS * KT:
                        split(piece % 4, WO_Q + piece, TILES + piece // 4)
                    if b == 0 and k + MR < KT:
                        mix_hi(k + MR)
                    if b > 0 and k < 4:
                        square_y(4 * (b - 1) + k)
            for st in range(4):
                square_y(4 * (BLOCKS - 1) + st)
            act.wait_ge(y_rstd_ready, 2)
            act.wait_ge(y_weighted, 28)
            for st in (2, 3):
                act.activation(y_res[:, st, 0:3 * N], y_res[:, st, 0:3 * N], ACT.Copy,
                               scale=y_rstd[:, st:st + 1]).then_inc(y_final_act, 1)

        @block.vector
        def _(dve):
            def split(quarter, slot):
                dve.wait_ge(w_hi_ready, quarter + 1)
                dve.tensor_tensor(w_lo[:, slot, :], w_raw[:, slot, :], w_hi[:, slot, :], ALU.subtract
                                  ).then_inc(w_lo_ready, 1)

            dve.memset(zeros, 0.0).then_inc(zeros_ready, 1)

            def normalise_x(t):
                dve.wait_ge(x_squared, t + 1)
                dve.tensor_scalar(x_var[:, t:t + 1], x_ssq[:, t:t + 1], 1.0 / D, EPS, ALU.mult, ALU.add
                                  ).then_inc(x_var_ready, 1)
                dve.wait_ge(x_weighted, t + 1)
                dve.wait_ge(x_rstd_ready, t + 1)
                dve.tensor_scalar(x_tile[t % XR], x_tile[t % XR], x_rstd[:, t:t + 1], None, ALU.mult
                                  ).then_inc(x_normed, 1)

            normalise_x(0)
            for t in range(ST):
                if t + 1 < ST:
                    normalise_x(t + 1)
                for b in range(4):
                    dve.wait_ge(hn_hi_ready, 4 * t + b + 1)
                    dve.tensor_tensor(act_lo[:, 4 * b:4 * b + 4, t * P:(t + 1) * P],
                                      banks[:, turn_bank(t, b), :].rearrange("p (k s) -> p k s", k=4),
                                      act_hi[:, 4 * b:4 * b + 4, t * P:(t + 1) * P], ALU.subtract
                                      ).then_inc(hn_lo_ready, 1)
                if 0 <= t <= 3:
                    split(t, t)
            dve.wait_ge(taps_turned, 1)
            dve.tensor_copy(taps[:, :, :].rearrange("p t g -> p (t g)"), banks[:, 7, 0:(TAPS + 1) * GROUPS]
                            ).then_inc(taps_copied, 1)
            dve.wait_ge(taps_turned, 2)
            dve.tensor_copy(rel_tab, banks[0:HEADS, 6, 0:REL]).then_inc(rel_copied, 1)
            dve.wait_ge(x_turned, 4 * ST)
            dve.wait_ge(x_squared, ST)
            dve.memset(u_buf[:, 0:2], 0.0).then_inc(u_zeroed, 1)
            for kv in range(KVH):
                dve.memset(logits[kv][:, :, 0:CHUNK], NEG).then_inc(neg_written, 1)
            dve.wait_ge(small_loaded, 16 * 7)
            for kv in range(KVH):
                for par in range(2):
                    rows = slice(par * CHUNK, (par + 1) * CHUNK)
                    sink = sink_row[rows, :].rearrange("p (v j a) -> p v j a", v=KVH, a=2)[:, kv, :, par]
                    dve.tensor_copy(logits[kv][rows, :, BAND], sink).then_inc(sinks_placed, 1)

            def stage_lo(tile, par):
                dve.wait_ge(hi_staged, tile + 1)
                dve.tensor_tensor(stage[:, 1, :].bitcast(F32R).rearrange("p (a s) -> p a s", a=2),
                                  proj[par], stage[:, 0, :].rearrange("p (a s) -> p a s", a=2), ALU.subtract
                                  ).then_inc(proj_free, 1)

            def silu(out_ap, count, par):
                dve.wait_ge(gate_exp, count)
                dve.tensor_scalar(h_buf, h_buf, 1.0, None, ALU.add).then_inc(gate_divisor, 1)
                dve.wait_ge(gate_divisor, count)
                dve.reciprocal(h_buf, h_buf).then_inc(sigmoid_ready, 1)
                dve.wait_ge(sigmoid_ready, count)
                dve.tensor_tensor(out_ap.rearrange("p (a s) -> p a s", a=2), proj[par],
                                  h_buf.rearrange("p (a s) -> p a s", a=2), ALU.mult).then_inc(proj_free, 1)

            def attn_gate(tile, par, first=False):
                if not first:
                    dve.wait_ge(gate_stored, (tile - QKV_TILES) * 16)
                silu(y_buf, tile - (QKV_TILES - 1), par)

            def splits(e, middle=None):
                split(e * 4 + 3, 3)
                if middle:
                    middle()
                for q in range(3):
                    split(e * 4 + 4 + q, q)

            for q in range(3):
                split(4 + q, q)
            with dve.Fori(0, QKV_TILES // 2) as i:
                for par in range(2):
                    splits(i * 2 + (1 + par), lambda: stage_lo(i * 2 + par, par))

            def gate_pair(i, first):
                for par in range(2):
                    splits(i * 2 + (1 + par), lambda: attn_gate(i * 2 + par, par, first and par == 0))

            gate_pair(QKV_TILES // 2, True)
            with dve.Fori(QKV_TILES // 2 + 1, A_TILES // 2 - 1) as i:
                gate_pair(i, False)
            splits(A_TILES - 1, lambda: attn_gate(A_TILES - 2, 0))
            dve.wait_ge(bias_loaded, 32)

            def shift_logits(unit, kv, first_chunk):
                dve.wait_ge(qk_done, unit + 1)
                lo = CHUNK if first_chunk else 0
                dve.scalar_tensor_tensor(out=logits[kv][:, :, lo:BAND],
                                         in0=logit_ps.rearrange("p (j k) -> p j k", j=PAIRS)[:, :, lo:],
                                         scalar=SCALE, in1=bias[:, kv * PAIRS:(kv + 1) * PAIRS, lo:],
                                         op0=ALU.mult, op1=ALU.add).then_inc(logits_read, 1)
                dve.wait_ge(logits_read, unit + 1)
                if first_chunk:
                    dve.wait_ge(neg_written, KVH)
                    dve.wait_ge(sinks_placed, 2 * KVH)
                dve.tensor_reduce(row_max, logits[kv], AX_X, ALU.max).then_inc(max_ready, 1)
                dve.wait_ge(max_ready, unit + 1)
                if not (isinstance(unit, int) and unit == 0):
                    dve.wait_ge(probs_turned, unit)
                dve.tensor_tensor(probs, logits[kv], row_max.unsqueeze(2).to_broadcast([P, PAIRS, LW]),
                                  ALU.subtract).then_inc(shifted, 1)

            def normalise(unit):
                dve.wait_ge(exp_done, unit + 1)
                dve.tensor_reduce(row_sum, probs, AX_X, ALU.add).then_inc(sum_ready, 1)
                dve.wait_ge(sum_ready, unit + 1)
                dve.reciprocal(row_inv, row_sum).then_inc(inv_ready, 1)
                dve.wait_ge(inv_ready, unit + 1)
                dve.tensor_tensor(probs[:, :, 0:BAND], probs[:, :, 0:BAND],
                                  row_inv.unsqueeze(2).to_broadcast([P, PAIRS, BAND]), ALU.mult
                                  ).then_inc(probs_ready, 1)

            def gate_output(unit, first):
                dve.wait_ge(pv_done, unit + 1)
                dve.wait_ge(g_loaded, unit * 16 + 16)
                if not first:
                    dve.wait_ge(o_stored, unit * 16)
                o = o_ps.rearrange("p (j a k) -> p j a k", j=PAIRS, a=2)
                for par in range(2):
                    rows = slice(par * HEAD, (par + 1) * HEAD)
                    op = dve.tensor_tensor(o_mix[rows, :, :], o[rows, :, par, :], g_cur[rows, :, :], ALU.mult)
                op.then_inc(o_ready, 1)

            def halves(ap):
                return ap.rearrange("p (a s) -> p a s", a=2)

            def conv_h(g, e):
                dve.wait_ge(w_free, e * 4 + 8)
                dve.tensor_copy(halves(h_buf), proj[0]).then_inc(proj_free, 1)

            def conv_c(g, e, first):
                dve.wait_ge(w_free, e * 4 + 8)
                dve.wait_ge(proj_free, e + 2)
                dve.tensor_tensor(halves(u_buf[:, 2:]), proj[1], halves(h_buf), ALU.mult).then_inc(proj_free, 1)
                dve.wait_ge(proj_free, e + 3)
                if first:
                    dve.wait_ge(gate_stored, 16 * (A_TILES - QKV_TILES))
                    dve.wait_ge(u_zeroed, 1)
                else:
                    dve.wait_ge(conv_stored, g * 16)
                dve.tensor_scalar(y_buf, u_buf[:, 2:2 + S], tap_ap(2, g), tap_ap(3, g), ALU.mult, ALU.add
                                  ).then_inc(conv_step, 1)
                for t in (1, 0):
                    dve.wait_ge(conv_step, g * 4 + 2 - t)
                    dve.scalar_tensor_tensor(out=y_buf, in0=u_buf[:, t:t + S], scalar=tap_ap(t, g), in1=y_buf,
                                             op0=ALU.mult, op1=ALU.add).then_inc(conv_step, 1)

            def tap_ap(t, g):
                return taps[:, t, bass.ds(g, 1)]

            def conv_gate(g, e):
                dve.wait_ge(conv_step, g * 4 + 3)
                silu(u_buf[:, 2:], g + (A_TILES - QKV_TILES + 1), 0)
                dve.wait_ge(proj_free, e + 3)
                dve.tensor_tensor(y_buf, y_buf, u_buf[:, 2:], ALU.mult).then_inc(conv_step, 1)

            def conv_b_gate(g, e):
                dve.wait_ge(w_free, e * 4 + 8)
                dve.wait_ge(conv_step, g * 4 + 4)
                dve.tensor_tensor(halves(y_buf), proj[1], halves(y_buf), ALU.mult).then_inc(proj_free, 1)

            def mix_lo(t):
                dve.wait_ge(mix_hi_ready, t + 1)
                dve.tensor_tensor(act_lo[:, t, :], mix_raw[t % MR], act_hi[:, t, :], ALU.subtract
                                  ).then_inc(mix_lo_ready, 1)

            def group(g, first, last):
                for kind in range(4):
                    e = g * 4 + A_TILES + kind
                    unit = g * 4 + kind
                    if not (first and kind == 0):
                        gate_output(unit - 1, first and kind == 1)
                    shift_logits(unit, kind % 2, first and kind < 2)
                    split(e * 4 + 3, 3)
                    normalise(unit)
                    split(e * 4 + 4, 0)
                    if kind == 0:
                        if first:
                            attn_gate(A_TILES - 1, 1)
                        else:
                            conv_b_gate(g - 1, e - 1)
                    elif kind == 1:
                        conv_h(g, e - 1)
                    elif kind == 2:
                        conv_c(g, e - 1, first)
                    else:
                        conv_gate(g, e - 1)
                    dve.wait_ge(pt_hi_ready, unit + 1)
                    dve.tensor_tensor(pt_lo[:, :], pt_ps, pt_hi[:, :], ALU.subtract).then_inc(pt_lo_ready, 1)
                    split(e * 4 + 5, 1)
                    if last and kind == 3:
                        mix_lo(0)
                    split(e * 4 + 6, 2)
                    if last and kind == 3:
                        for t in range(1, MR):
                            mix_lo(t)

            group(0, True, False)
            with dve.Fori(1, GROUPS - 1) as g:
                group(g, False, False)
            group(GROUPS - 1, False, True)

            gate_output(UNITS - 1, False)
            conv_b_gate(GROUPS - 1, TILES - 1)

            def add_resid(r):
                b, st = r // 4, r % 4
                if st < 3:
                    dve.wait_ge(out_done, 3 * b + st + 1)
                else:
                    dve.wait_ge(w_free, WO_Q + 4 + (b + 1) * KT)
                dve.wait_ge(resid_loaded[r % 2], 16 * (r // 2 + 1))
                if r == 0:
                    dve.wait_ge(conv_stored, 16 * GROUPS)
                    dve.wait_ge(o_stored, 16 * UNITS)
                if r == 16:
                    dve.wait_ge(out_stored, 16 * 4)
                dve.tensor_tensor(y_res[:, st, (b % 4) * N:(b % 4 + 1) * N], banks[:, 4 - 4 * (b % 2) + st, :],
                                  resid[:, r % 2, :], ALU.add).then_inc(y_ready, 1)

            def final_rstd(half):
                dve.wait_ge(bank_free, 8 + 16 * (half + 1))
                dve.tensor_reduce(y_ssq, ssq[:, :, :], AX_X, ALU.add).then_inc(y_ssq_ready, 1)
                dve.wait_ge(y_ssq_ready, half + 1)
                dve.tensor_scalar(y_var, y_ssq, 1.0 / D, EPS, ALU.mult, ALU.add).then_inc(y_var_ready, 1)
                dve.wait_ge(y_rstd_ready, half + 1)

            def scale_rows(st, end):
                dve.tensor_scalar(y_res[:, st, 0:end], y_res[:, st, 0:end], y_rstd[:, st:st + 1], None, ALU.mult
                                  ).then_inc(y_final, 1)

            def finish_last_block(st):
                cols = slice(3 * N, 4 * N)
                dve.scalar_tensor_tensor(out=y_res[:, st, cols], in0=y_res[:, st, cols],
                                         scalar=y_rstd[:, st:st + 1], in1=final_row[:, cols],
                                         op0=ALU.mult, op1=ALU.mult).then_inc(y_last_final, 1)

            for b in range(BLOCKS):
                for k in range(KT):
                    piece = b * KT + k + 3
                    if piece < BLOCKS * KT:
                        split(WO_Q + piece, piece % 4)
                    if b == 0 and k + MR < KT:
                        mix_lo(k + MR)
                    if b > 0 and k < 4:
                        add_resid(4 * (b - 1) + k)
                    if b == 4 and 4 <= k < 8:
                        if k == 4:
                            final_rstd(0)
                            dve.wait_ge(y_weighted, 16)
                        scale_rows(k - 4, D)
            for st in range(4):
                add_resid(4 * (BLOCKS - 1) + st)
            final_rstd(1)
            dve.wait_ge(final_row_loaded, 16)
            dve.wait_ge(y_weighted, 28)
            for st in range(4):
                if st < 2:
                    scale_rows(st, 3 * N)
                finish_last_block(st)

        @block.tensor
        def _(pe):
            def turn_x(t):
                pe.wait_ge(x_normed, t + 1)
                for b in range(4):
                    before = t - 2 if t < 4 else t - 1
                    if before >= 0:
                        pe.wait_ge(hn_lo_ready, 4 * before + b + 1)
                    for j in range(4):
                        k = 4 * b + j
                        op = pe.transpose(banks[:, turn_bank(t, b), j * P:(j + 1) * P],
                                          x_tile[t % XR][:, k * P:(k + 1) * P], ident[:, :])
                    op.then_inc(x_turned, 1)

            def quarter(q, count, par, halves=(0, 1)):
                pe.wait_ge(w_lo_ready, count + 1)
                for j in range(QK):
                    k = q * QK + j
                    wh = w_hi[:, q, j * P:(j + 1) * P]
                    wl = w_lo[:, q, j * P:(j + 1) * P]
                    for w, a in ((wh, act_hi), (wh, act_lo), (wl, act_hi)):
                        for s in halves:
                            op = pe.matmul(proj[par][:, s, :], w, a[:, k, s * N:(s + 1) * N],
                                           start=(k == 0 and w is wh and a is act_hi),
                                           stop=(k == KT - 1 and w is wl))
                return op

            pe.wait_ge(ident_ready, 1)
            for t in range(4):
                turn_x(t)
            pe.wait_ge(proj_free, 1)
            for q in range(4):
                if q == 0:
                    pe.wait_ge(hn_lo_ready, 4 * 4)
                quarter(q, q, 0, (0,))
                turn_x(4 + q)
            pe.wait_ge(hn_lo_ready, 4 * ST)
            pe.wait_ge(small_loaded, 16 * 7)
            rows = (TAPS + 1) * GROUPS
            pe.transpose(banks[:, 7, 0:rows], tap_rows, ident[0:rows, 0:rows]).then_inc(taps_turned, 1)
            pe.matmul(banks[0:HEADS, 6, 0:REL], rel_rows, hot_rows, start=True, stop=True
                      ).then_inc(taps_turned, 1)
            for q in range(4):
                quarter(q, q, 0, (1,)).then_inc(w_free, 1)

            def column_tile(i, par):
                pe.wait_ge(proj_free, i * 2 + (par + 1))
                for q in range(4):
                    quarter(q, i * 8 + (4 * par + q), par).then_inc(w_free, 1)

            column_tile(0, 1)
            with pe.Fori(1, A_TILES // 2) as i:
                for par in range(2):
                    column_tile(i, par)

            with pe.Fori(0, GROUPS) as g:
                for kind in range(4):
                    e = g * 4 + (A_TILES + kind)
                    unit = g * 4 + kind
                    kv = kind % 2
                    pe.wait_ge(qk_loaded, unit * 64 + 64)
                    for j in range(PAIRS):
                        for c in range(2):
                            op = pe.matmul(logit_ps[:, j * BAND:(j + 1) * BAND],
                                           q_cur[:, 2 * j:2 * j + 2, :].rearrange("p h s -> p (h s)"),
                                           k_cur[:, c, :], start=(c == 0), stop=(c == 1))
                    op.then_inc(qk_done, 1)
                    pe.wait_ge(proj_free, e + 1)
                    quarter(0, e * 4, kind % 2).then_inc(w_free, 1)
                    if kv == 0:
                        pe.wait_ge(v_loaded, (g * 2 + kind // 2) * 16 + 16)
                        for c in range(2):
                            op = pe.transpose(v_ps[:, c * P:(c + 1) * P], v_win[:, c, :], ident[:, :])
                        op.then_inc(v_turned, 1)
                    quarter(1, e * 4 + 1, kind % 2).then_inc(w_free, 1)
                    pe.wait_ge(probs_ready, unit + 1)
                    for j in range(PAIRS):
                        op = pe.transpose(pt_ps[:, j * P:(j + 1) * P], probs[:, j, 0:BAND], ident[:, :])
                    op.then_inc(probs_turned, 1)
                    quarter(2, e * 4 + 2, kind % 2).then_inc(w_free, 1)
                    quarter(3, e * 4 + 3, kind % 2).then_inc(w_free, 1)
                    pe.wait_ge(pt_lo_ready, unit + 1)
                    pe.wait_ge(v_ready, g * 2 + (kind // 2 + 1))
                    vh, vl = (v_cur[:, c, kv, :, :].rearrange("p a d -> p (a d)") for c in range(2))
                    for i, (v, pt) in enumerate(((vh, pt_hi), (vh, pt_lo), (vl, pt_hi))):
                        op = pe.matmul(o_ps, v, pt[:, :], start=(i == 0), stop=(i == 2))
                    op.then_inc(pv_done, 1)

            def out_block(b, par, half, first):
                for k in range(KT):
                    pe.wait_ge(w_lo_ready, b * KT + (WO_Q + k + 1))
                    if first:
                        pe.wait_ge(mix_lo_ready, k + 1)
                    for st in range(4):
                        tok = slice(half * N + st * P, half * N + (st + 1) * P)
                        if k == 0:
                            pe.wait_ge(bank_free, b * 4 + (st + 1))
                            if first and par == 0 and st == 0:
                                pe.wait_ge(v_ready, NC)
                            if first and par == 0 and st == 3:
                                pe.wait_ge(o_ready, UNITS)
                            if first and par == 1 and st == 0:
                                pe.wait_ge(proj_free, TILES + 2)
                        bank = banks[:, 4 - 4 * par + st, :]
                        for i, (a, w) in enumerate(((act_hi, w_hi), (act_hi, w_lo), (act_lo, w_hi))):
                            op = pe.matmul(bank, a[:, k, tok], w[:, k % 4, :], start=(k == 0 and i == 0),
                                           stop=(k == KT - 1 and i == 2))
                        if k == KT - 1 and st < 3:
                            op.then_inc(out_done, 1)
                    op.then_inc(w_free, 1)

            for half in range(SH):
                with pe.Fori(half * 2, half * 2 + 2) as i:
                    for par in range(2):
                        out_block(i * 2 + par, par, half, half == 0)


_INS = ["x", "norm_w", "w_in", "sinks", "conv_w", "conv_b", "w_out", "rel_bias", "final_norm_w"]


def kernel(**inputs):
    import numpy as _np
    import concourse.bacc as _bacc
    from concourse import mybir as _mybir
    from concourse.bass_utils import run_bass_kernel_spmd as _run

    nc = _bacc.Bacc("TRN2", target_bir_lowering=False, num_devices=1)
    given = {name: _np.ascontiguousarray(inputs[name]) for name in _INS}
    given["one_hot"] = t5_one_hot()
    arrays, args = {}, []
    for name, a in given.items():
        arrays[f"in_{name}_dram"] = a
        args.append(nc.dram_tensor(f"in_{name}_dram", a.shape, _mybir.dt.from_np(a.dtype), kind="ExternalInput").ap())
    args.append(nc.dram_tensor("out_0_dram", (1, S, D), F32, kind="ExternalOutput").ap())
    build(nc, *args)
    r = _run(nc, [arrays], core_ids=[0])
    return r.results[0]["out_0_dram"]
```

```python
import math
from contextlib import ExitStack

import numpy as np
import concourse.bass as bass
from concourse import mybir

F32 = mybir.dt.float32
F32R = mybir.dt.float32r
ALU = mybir.AluOpType
ACT = mybir.ActivationFunctionType
AX_X = mybir.AxisListType.X

P = 128
D = 2048
S = 1024
CHUNK = 64
HEAD = 64
BAND = 2 * CHUNK
HEADS = 16
KVH = 2
PAIRS = HEADS // KVH // 2
ATTN = HEADS * HEAD
CONV = 1024
TAPS = 3
BUCKETS = 32
MAX_DISTANCE = 128
EPS = 1e-6
NEG = -1e30
SCALE = 1.0 / math.sqrt(HEAD)

KT = D // P
QK = KT // 4
ST = S // P
NC = S // CHUNK
N = 512
SH = S // N
QKV_TILES = (ATTN + 2 * KVH * HEAD) // P
K_ROW = ATTN
V_ROW = ATTN + KVH * HEAD
A_TILES = QKV_TILES + ATTN // P
GROUPS = CONV // P
TILES = A_TILES + 4 * GROUPS
UNITS = NC * KVH
REL = 192
XR = 4
POOL_TILES = (3, 4, 6)
MR = 8
LR = 4
BLOCKS = SH * (D // N)
WO_Q = 4 * TILES
RING_PIECES = (BLOCKS - 1) * KT


def t5_one_hot():
    rel = np.arange(REL) - (BAND - 1)
    n = -rel
    half = BUCKETS // 2
    ret = (n < 0).astype(np.int32) * half
    n = np.abs(n)
    max_exact = half // 2
    nf = np.maximum(n, 1).astype(np.float32)
    large = max_exact + (np.log(nf / max_exact) / math.log(MAX_DISTANCE / max_exact)
                         * (half - max_exact)).astype(np.int32)
    large = np.minimum(large, half - 1)
    bucket = ret + np.where(n < max_exact, n, large).astype(np.int32)
    return (bucket[None, :] == np.arange(BUCKETS)[:, None]).astype(np.float32)


def build(nc, x, norm_w, w_in, sinks, conv_w, conv_b, w_out, rel_bias, final_norm_w, one_hot, out):
    ctx = ExitStack()
    with ctx:
        def sb(name, shape, dt=F32):
            return ctx.enter_context(nc.sbuf_tensor(name, shape, dt))

        def sem(name):
            return ctx.enter_context(nc.semaphore(name))

        qkv_park = nc.dram_tensor("qkv_park", [2, QKV_TILES * P, CHUNK + S], F32, kind="Internal").ap()
        gate_park = nc.dram_tensor("gate_park", [ATTN, S], F32, kind="Internal").ap()
        mix_park = nc.dram_tensor("mix_park", [ATTN + CONV, S], F32, kind="Internal").ap()
        rel_park = nc.dram_tensor("rel_park", [HEADS, CHUNK, REL], F32, kind="Internal").ap()

        act_hi = sb("act_hi", [P, KT, S], F32R)
        act_lo = sb("act_lo", [P, KT, S], F32R)
        w_raw = sb("w_raw", [P, 4, N])
        w_hi = sb("w_hi", [P, 4, N], F32R)
        w_lo = sb("w_lo", [P, 4, N], F32R)
        q_cur = sb("q_cur", [P, PAIRS * 2, CHUNK], F32R)
        k_cur = sb("k_cur", [P, 2, BAND], F32R)
        pt_hi = sb("pt_hi", [P, N], F32R)
        pt_lo = sb("pt_lo", [P, N], F32R)
        v_cur = sb("v_cur", [P, KVH, 3, HEAD], F32R)
        ident = sb("ident", [P, P])
        taps = sb("taps", [P, TAPS + 1, GROUPS])
        small = sb("small", [P, 68])
        ssq = sb("ssq", [P, 4, 4])

        arena = sb("arena", [P, 4 * D])
        stage = sb("stage", [P, 2, S])
        resid = sb("resid", [P, 2, N])

        off = [0]

        def carve(n):
            off[0] += n
            return arena[:, off[0] - n:off[0]]

        h_buf = carve(S)
        u_buf = carve(2 + S)
        y_buf = carve(S)
        bias = carve(HEADS // 2 * BAND).rearrange("p (j k) -> p j k", j=HEADS // 2)
        LW = BAND + 1
        logits = [carve(PAIRS * LW).rearrange("p (j k) -> p j k", j=PAIRS) for _ in range(KVH)]
        probs = carve(PAIRS * LW).rearrange("p (j k) -> p j k", j=PAIRS)
        v_win = carve(2 * BAND).rearrange("p (c k) -> p c k", c=2)
        g_cur = carve(PAIRS * CHUNK).rearrange("p (j k) -> p j k", j=PAIRS)
        o_mix = carve(PAIRS * CHUNK).rearrange("p (j k) -> p j k", j=PAIRS)
        o_lo = carve(PAIRS * CHUNK).rearrange("p (j k) -> p j k", j=PAIRS)
        assert off[0] <= 4 * D
        x_tile = [arena[:, i * D:(i + 1) * D] for i in range(XR)]
        norm_row = stage[:, :, :].rearrange("p a s -> p (a s)")
        square = act_hi[:, :, S - P:]
        setup = resid[:, :, :].rearrange("p a s -> p (a s)")
        tap_rows = setup[0:(TAPS + 1) * GROUPS, 0:P]
        rel_rows = setup[0:BUCKETS, P:P + HEADS]
        hot_rows = setup[0:BUCKETS, 256:256 + REL]
        rel_tab = setup[0:HEADS, 512:512 + REL]
        zeros = setup[:, 768:768 + CHUNK]
        spare = carve(S)
        mix_raw = [place[:, i * N:(i + 1) * N] for place in (stage[:, 0, :], stage[:, 1, :], setup, spare)
                   for i in range(2)]
        assert off[0] <= 4 * D
        y_res = arena[:, :].rearrange("p (t c) -> p t c", t=4)
        late_raw = [y_res[:, i, 3 * N:] for i in range(LR)]
        tail_hi = act_hi[:, :, 0:N]
        tail_lo = act_lo[:, :, 0:N]
        final_row = stage[:, :, :].rearrange("p a s -> p (a s)")

        row_max = small[:, 0:4]
        row_sum = small[:, 4:8]
        row_inv = small[:, 8:12]
        minus_half = small[:, 64:68]
        x_ssq = small[:, 12:20]
        x_var = small[:, 20:28]
        x_rstd = small[:, 28:36]
        y_ssq = small[:, 36:40]
        y_var = small[:, 40:44]
        y_rstd = small[:, 44:48]
        sink_row = small[:, 48:64]

        banks = ctx.enter_context(nc.psum_tensor("banks", [P, 8, N], F32))
        proj = [banks[:, 0:2, :], banks[:, 2:4, :]]
        v_ps, pt_ps = (banks[:, b, :] for b in (4, 6))
        o_ps = banks[:, 7, :].rearrange("p (a j k) -> p a j k", a=2, j=PAIRS)
        logit_ps = banks[:, 5:7, :].rearrange("p b (j c k) -> p (b j) c k", j=PAIRS // 2, c=2)

        ident_zero = sem("ident_zero")
        minus_half_ready = sem("minus_half_ready")
        ident_ready = sem("ident_ready")
        small_loaded = sem("small_loaded")
        u_zeroed = sem("u_zeroed")
        zeros_ready = sem("zeros_ready")
        pad_stored = sem("pad_stored")
        taps_turned = sem("taps_turned")
        taps_copied = sem("taps_copied")
        rel_copied = sem("rel_copied")
        rel_stored = sem("rel_stored")
        bias_loaded = sem("bias_loaded")
        neg_written = sem("neg_written")
        sinks_placed = sem("sinks_placed")
        norm_row_loaded = sem("norm_row_loaded")
        x_loaded = [sem(f"x_loaded{i}") for i in range(XR)]
        x_squared = sem("x_squared")
        x_var_ready = sem("x_var_ready")
        x_rstd_ready = sem("x_rstd_ready")
        x_weighted = sem("x_weighted")
        x_normed = sem("x_normed")
        x_turned = sem("x_turned")
        hn_hi_ready = sem("hn_hi_ready")
        hn_lo_ready = sem("hn_lo_ready")
        raw_loaded = [sem(f"raw_loaded{i}") for i in range(4)]
        w_hi_ready = sem("w_hi_ready")
        w_lo_ready = sem("w_lo_ready")
        w_free = sem("w_free")
        proj_free = sem("proj_free")
        hi_staged = sem("hi_staged")
        qkv_stored = sem("qkv_stored")
        gate_exp = sem("gate_exp")
        gate_divisor = sem("gate_divisor")
        sigmoid_ready = sem("sigmoid_ready")
        gate_stored = sem("gate_stored")
        conv_step = sem("conv_step")
        conv_stored = sem("conv_stored")
        qk_loaded = sem("qk_loaded")
        v_loaded = sem("v_loaded")
        g_loaded = sem("g_loaded")
        qk_done = sem("qk_done")
        logits_read = sem("logits_read")
        max_ready = sem("max_ready")
        shifted = sem("shifted")
        exp_done = sem("exp_done")
        sum_ready = sem("sum_ready")
        inv_ready = sem("inv_ready")
        probs_ready = sem("probs_ready")
        probs_turned = sem("probs_turned")
        pt_hi_ready = sem("pt_hi_ready")
        pt_lo_ready = sem("pt_lo_ready")
        v_turned = sem("v_turned")
        v_ready = sem("v_ready")
        pv_done = sem("pv_done")
        o_lo_ready = sem("o_lo_ready")
        o_summed = sem("o_summed")
        o_ready = sem("o_ready")
        o_stored = sem("o_stored")
        mix_loaded = [sem(f"mix_loaded{i}") for i in range(MR)]
        late_loaded = [sem(f"late_loaded{i}") for i in range(LR)]
        tail_hi_ready = sem("tail_hi_ready")
        tail_lo_ready = sem("tail_lo_ready")
        mix_hi_ready = sem("mix_hi_ready")
        mix_lo_ready = sem("mix_lo_ready")
        out_done = sem("out_done")
        bank_free = sem("bank_free")
        resid_loaded = [sem(f"resid_loaded{i}") for i in range(2)]
        y_ready = sem("y_ready")
        y_ssq_ready = sem("y_ssq_ready")
        y_var_ready = sem("y_var_ready")
        y_rstd_ready = sem("y_rstd_ready")
        final_row_loaded = sem("final_row_loaded")
        y_final = sem("y_final")
        y_weighted = sem("y_weighted")
        y_final_act = sem("y_final_act")
        out_stored = sem("out_stored")
        out_stored_last = sem("out_stored_last")

        w_in_v = w_in[0].rearrange("(k p) c -> p k c", p=P)
        w_out_v = w_out[0].rearrange("(k p) c -> p k c", p=P)
        x_v = x[0].rearrange("(t p) d -> p t d", p=P)
        out_v = out[0].rearrange("(t p) d -> p t d", p=P)
        qkv_v = qkv_park.rearrange("c (m p) s -> p c m s", p=P)
        qkv_head = qkv_park.rearrange("c (h d) s -> d c h s", d=HEAD)
        gate_v = gate_park.rearrange("(m p) s -> p m s", p=P)
        mix_v = mix_park.rearrange("(m p) s -> p m s", p=P)

        def mix_row_tile(t):
            return (t + ATTN // P) % KT

        def conv_col(kind, g):
            return A_TILES * P + (0, 1, 3, 2)[kind] * CONV + g * P

        TURN_BANKS = [4, 5, 6, 7, 0, 1, 2, 3, 4, 5, 6, 7, 1, 2, 3, 4] + [5, 6, 7, 2, 3, 4, 5, 6, 7, 2, 3, 4, 5, 6, 7, 2]

        def turn_bank(t, b):
            return TURN_BANKS[4 * t + b]

        block = ctx.enter_context(nc.Block())

        @block.sync
        def _(sp):
            def at(column):
                return column if isinstance(column, int) else sp.snap(column)

            def load_in(slot, quarter, col):
                col = at(col)
                if not (isinstance(quarter, int) and quarter < 4):
                    sp.wait_ge(w_lo_ready, quarter - 3)
                sp.dma_start(w_raw[:, slot, :].rearrange("p (k c) -> p k c", k=QK),
                             w_in_v[:, slot * QK:(slot + 1) * QK, bass.ds(col, P)]
                             ).then_inc(raw_loaded[slot], 16)

            def load_out(slot, piece, row_tile, dblk):
                sp.wait_ge(w_lo_ready, WO_Q + piece - 3)
                sp.dma_start(w_raw[:, slot, :], w_out_v[:, row_tile, dblk * N:(dblk + 1) * N]
                             ).then_inc(raw_loaded[slot], 16)

            def load_qk(queries, band, kv):
                for c in range(2):
                    half = slice(c * HEAD, (c + 1) * HEAD)
                    sp.dma_start(q_cur[half, :, :].bitcast(F32),
                                 qkv_head[:, c, kv * PAIRS * 2:(kv + 1) * PAIRS * 2,
                                          bass.ds(queries, CHUNK)]).then_inc(qk_loaded, 16)
                    sp.dma_start(k_cur[half, :, :].bitcast(F32),
                                 qkv_head[:, :, K_ROW // HEAD + kv, bass.ds(band, BAND)]
                                 ).then_inc(qk_loaded, 16)

            def load_v(band):
                sp.dma_start(v_win, qkv_v[:, :, V_ROW // P, bass.ds(band, BAND)]).then_inc(v_loaded, 16)

            def load_mix(t):
                if t >= MR:
                    sp.wait_ge(mix_lo_ready, t - MR + 1)
                if t < GROUPS:
                    sp.wait_ge(conv_stored, 16 * (t + 1))
                else:
                    sp.wait_ge(o_stored, 16 * UNITS)
                sp.dma_start(mix_raw[t % MR], mix_v[:, mix_row_tile(t), 0:N]).then_inc(mix_loaded[t % MR], 16)

            def load_mix2(t):
                sp.wait_ge(mix_lo_ready, KT + max(0, t - LR + 1))
                sp.dma_start(late_raw[t % LR], mix_v[:, mix_row_tile(t), N:]).then_inc(late_loaded[t % LR], 16)

            def load_tail(k):
                if k == 0:
                    sp.wait_ge(out_stored, 16 * 4)
                if k >= LR:
                    sp.wait_ge(tail_lo_ready, k - LR + 1)
                sp.dma_start(late_raw[k % LR], w_out_v[:, mix_row_tile(k), (D // N - 1) * N:]
                             ).then_inc(late_loaded[k % LR], 16)

            sp.dma_start(x_tile[0], x_v[:, 0, :]).then_inc(x_loaded[0], 16)
            sp.dma_start(norm_row, bass.AP(tensor=norm_w.tensor, offset=0, ap=[[0, P], [1, D]])
                         ).then_inc(norm_row_loaded, 16)
            for t in range(1, XR):
                sp.dma_start(x_tile[t], x_v[:, t, :]).then_inc(x_loaded[t], 16)
            for q in range(4):
                load_in(q, q, 0)
            for t in range(XR, ST):
                sp.wait_ge(x_turned, 4 * (t - XR + 1))
                sp.dma_start(x_tile[t % XR], x_v[:, t, :]).then_inc(x_loaded[t % XR], 16)
                if t == XR:
                    for i in range(TAPS):
                        sp.dma_start(tap_rows[i * GROUPS:(i + 1) * GROUPS, :],
                                     conv_w[0, i].rearrange("(g p) -> g p", p=P)).then_inc(small_loaded, 16)
                    sp.dma_start(tap_rows[TAPS * GROUPS:, :],
                                 conv_b[0].rearrange("(g p) -> g p", p=P)).then_inc(small_loaded, 16)
                    sp.dma_start(rel_rows, rel_bias).then_inc(small_loaded, 16)
                    sp.dma_start(hot_rows, one_hot).then_inc(small_loaded, 16)
                    sp.dma_start(sink_row, bass.AP(tensor=sinks.tensor, offset=0, ap=[[0, P], [1, HEADS]])
                                 ).then_inc(small_loaded, 16)
            for q in range(3):
                load_in(q, 4 + q, P)
            sp.wait_ge(rel_stored, 16)
            sp.wait_ge(hn_lo_ready, 4 * ST)
            for par in range(2):
                sp.dma_start(bias[par * CHUNK:(par + 1) * CHUNK, :, :],
                             bass.AP(tensor=rel_park.tensor, offset=par * CHUNK * REL + CHUNK - 1,
                                     ap=[[REL - 1, CHUNK], [2 * CHUNK * REL, HEADS // 2], [1, BAND]])
                             ).then_inc(bias_loaded, 16)

            with sp.Fori(0, A_TILES - 1) as e:
                load_in(3, e * 4 + 7, e * P + P)
                for q in range(3):
                    load_in(q, e * 4 + 8 + q, e * P + 2 * P)
            sp.wait_ge(qkv_stored, 32 * QKV_TILES)
            sp.wait_ge(pad_stored, 64)
            load_qk(CHUNK, 0, 0)
            load_v(0)
            e = A_TILES - 1
            load_in(3, 4 * e + 7, conv_col(0, 0))
            for q in range(3):
                load_in(q, 4 * e + 8 + q, conv_col(1, 0))

            def group(g, last):
                for kind in range(4):
                    e = g * 4 + A_TILES + kind
                    unit = g * 4 + kind
                    if not (last and kind == 3):
                        band = at((g * 2 + (kind + 1) // 2) * CHUNK)
                        queries = at((g * 2 + (kind + 1) // 2) * CHUNK + CHUNK)
                        sp.wait_ge(qk_done, unit + 1)
                        load_qk(queries, band, (kind + 1) % 2)

                    def raw(k):
                        ahead = kind + (1 if k == 0 else 2)
                        slot = (3 + k) % 4
                        if last and ahead >= 4:
                            piece = 4 * (ahead - 4) + slot
                            load_out(slot, piece, mix_row_tile(piece), 0)
                        else:
                            load_in(slot, e * 4 + 7 + k, conv_col(ahead % 4, g + ahead // 4))

                    raw(0)
                    raw(1)
                    if kind % 2 == 0 and not (last and kind == 2):
                        band = at((g * 2 + kind // 2 + 1) * CHUNK)
                        sp.wait_ge(v_turned, g * 2 + kind // 2 + 1)
                        load_v(band)
                    if last and kind == 3:
                        for t in range(GROUPS - 1):
                            load_mix(t)
                    raw(2)
                    raw(3)

            group(0, False)
            with sp.Fori(1, GROUPS - 1) as g:
                group(g, False)
            group(GROUPS - 1, True)

            def load_resid(r):
                half, dblk, st = r // 16, r // 4 % 4, r % 4
                if r >= 2:
                    sp.wait_ge(y_ready, r - 1)
                sp.dma_start(resid[:, r % 2, :], x_v[:, half * 4 + st, dblk * N:(dblk + 1) * N]
                             ).then_inc(resid_loaded[r % 2], 16)

            def store_last(st):
                sp.wait_ge(y_final, 4 + st + 1)
                sp.dma_start(out_v[:, 4 + st, 2 * N:], y_res[:, st, 2 * N:]).then_inc(out_stored_last, 16)
                sp.wait_ge(y_final_act, st + 1)
                sp.dma_start(out_v[:, 4 + st, 0:2 * N], y_res[:, st, 0:2 * N]).then_inc(out_stored_last, 16)

            for b in range(BLOCKS - 1):
                for k in range(KT):
                    ahead = b * KT + k + 7
                    if b > 0 and k in (2, 3):
                        load_resid(4 * b - 4 + k)
                    if ahead < RING_PIECES:
                        load_out(ahead % 4, ahead, mix_row_tile(ahead % KT), ahead // KT % 4)
                    if b == 0 and k + GROUPS - 1 < KT:
                        load_mix(k + GROUPS - 1)
                    if b in (1, 2) and k % 2 == 0:
                        load_mix2((b - 1) * GROUPS + k // 2)
                    if b in (5, 6) and k % 2 == 0:
                        load_tail((b - 5) * GROUPS + k // 2)
                    if k == KT - 2:
                        if b == 0:
                            sp.wait_ge(mix_lo_ready, KT - 2)
                            sp.dma_start(final_row, bass.AP(tensor=final_norm_w.tensor, offset=0,
                                                            ap=[[0, P], [1, D]])).then_inc(final_row_loaded, 16)
                        load_resid(4 * b)
                        load_resid(4 * b + 1)
            for r in range(4 * BLOCKS - 6, 4 * BLOCKS):
                load_resid(r)
                st = r - (4 * BLOCKS - 2)
                if st >= 0:
                    store_last(st)
            for st in (2, 3):
                store_last(st)
            sp.wait_ge(out_stored, 16 * 4)
            sp.wait_ge(out_stored_last, 16 * 8)

        @block.gpsimd
        def _(pool):
            pool.sem_inc(w_free, 4)
            pool.sem_inc(proj_free, 2)
            pool.sem_inc(bank_free, 8)
            pool.memset(ident[:, :], 0.0).then_inc(ident_zero, 1)
            pool.memset(minus_half, -0.5).then_inc(minus_half_ready, 1)
            pool.wait_ge(ident_zero, 1)
            pool.affine_select(out=ident[:, :], in_=ident[:, :], compare_op=ALU.not_equal, fill=1.0, base=0,
                               pattern=[[-1, P]], channel_multiplier=1).then_inc(ident_ready, 1)
            def x_inv_std(t):
                pool.wait_ge(x_var_ready, t + 1)
                pool.tensor_tensor(x_rstd[:, t:t + 1], x_var[:, t:t + 1], minus_half[:, 0:1], ALU.pow
                                   ).then_inc(x_rstd_ready, 1)

            def weight_x(t):
                pool.wait_ge(x_squared, t + 1)
                pool.tensor_tensor(x_tile[t % XR], x_tile[t % XR], norm_row, ALU.mult).then_inc(x_weighted, 1)

            pool.wait_ge(minus_half_ready, 1)
            pool.wait_ge(norm_row_loaded, 16)
            for t in range(3):
                x_inv_std(t)
            weight_x(3)
            x_inv_std(3)
            weight_x(4)
            x_inv_std(4)
            x_inv_std(5)
            weight_x(6)
            x_inv_std(6)
            x_inv_std(7)
            pool.wait_ge(zeros_ready, 1)
            for c in range(2):
                for m in (K_ROW // P, V_ROW // P):
                    pool.dma_start(qkv_v[:, c, m, 0:CHUNK], zeros).then_inc(pad_stored, 16)
            pool.wait_ge(rel_copied, 1)
            pool.dma_start(rel_park, rel_tab.unsqueeze(1).to_broadcast([HEADS, CHUNK, REL])).then_inc(rel_stored, 16)

            with pool.Fori(0, QKV_TILES) as m:
                pool.wait_ge(proj_free, m + 3)
                for c in range(2):
                    pool.dma_start(qkv_v[:, c, bass.ds(m, 1), CHUNK:].rearrange("p a s -> p (a s)"),
                                   stage[:, c, :]).then_inc(qkv_stored, 16)
            with pool.Fori(0, A_TILES - QKV_TILES) as m:
                pool.wait_ge(proj_free, m + (QKV_TILES + 3))
                pool.dma_start(gate_v[:, bass.ds(m, 1), :].rearrange("p a s -> p (a s)"), y_buf
                               ).then_inc(gate_stored, 16)
            with pool.Fori(0, GROUPS) as g:
                for kind in range(4):
                    pool.wait_ge(o_ready, g * 4 + kind + 1)
                    pool.dma_start(mix_v[:, (kind % 2) * PAIRS:(kind % 2 + 1) * PAIRS,
                                         bass.ds((g * 2 + kind // 2) * CHUNK, CHUNK)], o_mix
                                   ).then_inc(o_stored, 16)
                pool.wait_ge(proj_free, g * 4 + (A_TILES + 6))
                pool.dma_start(mix_v[:, bass.ds(g + ATTN // P, 1), :].rearrange("p a s -> p (a s)"), y_buf
                               ).then_inc(conv_stored, 16)
            def weight_y(r):
                b, st = r // 4, r % 4
                cols = slice((b % 4) * N, (b % 4 + 1) * N)
                pool.wait_ge(bank_free, 8 + r + 1)
                pool.tensor_tensor(y_res[:, st, cols], y_res[:, st, cols], final_row[:, cols], ALU.mult
                                   ).then_inc(y_weighted, 1)

            def final_rstd(count, cols):
                pool.wait_ge(y_var_ready, count)
                pool.tensor_tensor(y_rstd[:, cols], y_var[:, cols], minus_half[:, cols], ALU.pow
                                   ).then_inc(y_rstd_ready, 1)

            pool.wait_ge(final_row_loaded, 16)
            for r in range(16):
                weight_y(r)
            final_rstd(1, slice(0, 4))
            for st in range(4):
                pool.wait_ge(y_final, st + 1)
                pool.dma_start(out_v[:, st, :], y_res[:, st, :]).then_inc(out_stored, 16)
            for r in range(16, 28):
                weight_y(r)
            for st in range(4):
                final_rstd(2 + st, slice(st, st + 1))

        @block.scalar
        def _(act):
            def split(slot, quarter, turn):
                act.wait_ge(raw_loaded[slot], turn * 16 + 16)
                act.wait_ge(w_free, quarter + 1)
                act.activation(w_hi[:, slot, :], w_raw[:, slot, :], ACT.Copy).then_inc(w_hi_ready, 1)

            def square_x(t):
                act.wait_ge(x_loaded[t % XR], 16 * (t // XR + 1))
                if t >= 1:
                    act.wait_ge(x_squared, t)
                act.activation(square, x_tile[t % XR], ACT.Square, accum_out=x_ssq[:, t:t + 1]
                               ).then_inc(x_squared, 1)
                act.wait_ge(x_squared, t + 1)
                act.activation(x_var[:, t:t + 1], x_ssq[:, t:t + 1], ACT.Copy, scale=1.0 / D, bias=EPS
                               ).then_inc(x_var_ready, 1)

            def round_x(t):
                for b in range(4):
                    act.wait_ge(x_turned, 4 * t + b + 1)
                    act.activation(act_hi[:, 4 * b:4 * b + 4, t * P:(t + 1) * P],
                                   banks[:, turn_bank(t, b), :].rearrange("p (k s) -> p k s", k=4), ACT.Copy
                                   ).then_inc(hn_hi_ready, 1)

            square_x(0)
            square_x(1)
            round_x(0)
            square_x(2)
            square_x(3)
            round_x(1)
            split(0, 0, 0)
            split(1, 1, 0)
            square_x(4)
            round_x(2)
            split(2, 2, 0)
            split(3, 3, 0)
            round_x(3)
            square_x(5)
            square_x(6)
            square_x(7)
            for t in range(4, ST):
                round_x(t)

            def stage_hi(e, par, first):
                act.wait_ge(w_free, e * 4 + 8)
                if not first:
                    act.wait_ge(qkv_stored, e * 32)
                act.activation(stage[:, 0, :].bitcast(F32R).rearrange("p (a s) -> p a s", a=2),
                               proj[par], ACT.Copy).then_inc(hi_staged, 1)

            def exp_gate(tile, par):
                act.wait_ge(w_free, tile * 4 + 8)
                act.wait_ge(proj_free, tile + 2)
                act.activation(h_buf.rearrange("p (a s) -> p a s", a=2), proj[par], ACT.Exp, scale=-1.0
                               ).then_inc(gate_exp, 1)

            def splits(e, middle=None):
                split(3, e * 4 + 3, e)
                if middle:
                    middle()
                for q in range(3):
                    split(q, e * 4 + 4 + q, e + 1)

            def qkv_pair(i, first):
                for par in range(2):
                    splits(i * 2 + (1 + par), lambda: stage_hi(i * 2 + par, par, first and par == 0))

            for q in range(3):
                split(q, 4 + q, 1)
            qkv_pair(0, True)
            with act.Fori(1, QKV_TILES // 2) as i:
                qkv_pair(i, False)
            with act.Fori(QKV_TILES // 2, A_TILES // 2 - 1) as i:
                for par in range(2):
                    splits(i * 2 + (1 + par), lambda: exp_gate(i * 2 + par, par))
            splits(A_TILES - 1, lambda: exp_gate(A_TILES - 2, 0))

            def move_o_lo(count):
                act.wait_ge(pv_done, count)
                for par in range(2):
                    rows, other = (slice(i * HEAD, (i + 1) * HEAD) for i in (par, 1 - par))
                    op = act.activation(o_lo[rows, :, :], o_ps[other, par, :, :], ACT.Copy)
                op.then_inc(o_lo_ready, 1)

            def group(g, last):
                for kind in range(4):
                    e = g * 4 + A_TILES + kind
                    unit = g * 4 + kind
                    if not (isinstance(g, int) and g == 0 and kind == 0):
                        move_o_lo(unit)
                    act.wait_ge(shifted, unit + 1)
                    act.activation(probs, probs, ACT.Exp).then_inc(exp_done, 1)
                    split(3, e * 4 + 3, e)
                    if kind == 3:
                        exp_gate(e - 1, 0)
                    elif isinstance(g, int) and g == 0 and kind == 0:
                        exp_gate(e - 1, 1)
                    split(0, e * 4 + 4, e + 1)
                    if kind % 2 == 0:
                        n = g * 2 + kind // 2
                        act.wait_ge(v_turned, n + 1)
                        for i, c in enumerate((0, 1, 0)):
                            op = act.activation(v_cur[:, :, i, :],
                                                v_ps[:, c * P:(c + 1) * P].rearrange("p (h d) -> p h d", h=KVH),
                                                ACT.Copy)
                        op.then_inc(v_ready, 1)
                    act.wait_ge(probs_turned, unit + 1)
                    act.activation(pt_hi[:, :], pt_ps, ACT.Copy).then_inc(pt_hi_ready, 1)
                    if isinstance(g, int) and g == 0 and kind == 0:
                        act.wait_ge(gate_stored, 16 * (A_TILES - QKV_TILES))
                    act.dma_start(g_cur, gate_v[:, (kind % 2) * PAIRS:(kind % 2 + 1) * PAIRS,
                                                bass.ds((g * 2 + kind // 2) * CHUNK, CHUNK)]
                                  ).then_inc(g_loaded, 16)
                    split(1, e * 4 + 5, e + 1)
                    split(2, e * 4 + 6, e + 1)
                    if last and kind == 3:
                        for t in range(3):
                            mix_hi(t)

            def mix_hi(t):
                act.wait_ge(mix_loaded[t % MR], 16 * (t // MR + 1))
                act.wait_ge(w_free, 4 * TILES + t // 4 + 1)
                act.activation(act_hi[:, t, 0:N], mix_raw[t % MR], ACT.Copy).then_inc(mix_hi_ready, 1)

            def mix2_hi(t):
                act.wait_ge(late_loaded[t % LR], 16 * (t // LR + 1))
                act.activation(act_hi[:, t, N:], late_raw[t % LR], ACT.Copy).then_inc(mix_hi_ready, 1)

            def tail_split(k):
                act.wait_ge(late_loaded[k % LR], 16 * ((KT + k) // LR + 1))
                act.activation(tail_hi[:, k, :], late_raw[k % LR], ACT.Copy).then_inc(tail_hi_ready, 1)

            group(0, False)
            with act.Fori(1, GROUPS - 1) as g:
                group(g, False)
            group(GROUPS - 1, True)

            def square_y(r):
                act.wait_ge(y_ready, r + 1)
                b, st = r // 4, r % 4
                act.activation(banks[:, 4 - 4 * (b % 2) + st, :], y_res[:, st, (b % 4) * N:(b % 4 + 1) * N],
                               ACT.Square, accum_out=ssq[:, st, b % 4:b % 4 + 1]).then_inc(bank_free, 1)

            move_o_lo(UNITS)
            for b in range(BLOCKS):
                for k in range(KT):
                    piece = b * KT + k + 3
                    if piece < RING_PIECES:
                        split(piece % 4, WO_Q + piece, TILES + piece // 4)
                    if b == 0 and k + 3 < KT:
                        mix_hi(k + 3)
                    step = (b - 1) * KT + k
                    if step % 2 == 1 and 3 <= step < 2 * KT + 3:
                        mix2_hi((step - 3) // 2)
                    step = (b - 5) * KT + k
                    if step % 2 == 1 and 3 <= step < 2 * KT + 3:
                        tail_split((step - 3) // 2)
                    if b > 0 and k < 4:
                        square_y(4 * (b - 1) + k)
            act.wait_ge(y_weighted, 28)
            for st in range(4):
                square_y(4 * (BLOCKS - 1) + st)
                act.wait_ge(y_rstd_ready, 2 + st)
                act.activation(y_res[:, st, 0:2 * N], y_res[:, st, 0:2 * N], ACT.Copy,
                               scale=y_rstd[:, st:st + 1]).then_inc(y_final_act, 1)

        @block.vector
        def _(dve):
            def split(quarter, slot):
                dve.wait_ge(w_hi_ready, quarter + 1)
                dve.tensor_tensor(w_lo[:, slot, :], w_raw[:, slot, :], w_hi[:, slot, :], ALU.subtract
                                  ).then_inc(w_lo_ready, 1)

            dve.memset(zeros, 0.0).then_inc(zeros_ready, 1)

            def normalise_x(t):
                dve.wait_ge(x_rstd_ready, t + 1)
                if t in POOL_TILES:
                    dve.wait_ge(x_weighted, POOL_TILES.index(t) + 1)
                    dve.tensor_scalar(x_tile[t % XR], x_tile[t % XR], x_rstd[:, t:t + 1], None, ALU.mult
                                      ).then_inc(x_normed, 1)
                else:
                    dve.wait_ge(norm_row_loaded, 16)
                    dve.scalar_tensor_tensor(out=x_tile[t % XR], in0=x_tile[t % XR], scalar=x_rstd[:, t:t + 1],
                                             in1=norm_row, op0=ALU.mult, op1=ALU.mult).then_inc(x_normed, 1)

            def remainder_x(t):
                for b in range(4):
                    dve.wait_ge(hn_hi_ready, 4 * t + b + 1)
                    dve.tensor_tensor(act_lo[:, 4 * b:4 * b + 4, t * P:(t + 1) * P],
                                      banks[:, turn_bank(t, b), :].rearrange("p (k s) -> p k s", k=4),
                                      act_hi[:, 4 * b:4 * b + 4, t * P:(t + 1) * P], ALU.subtract
                                      ).then_inc(hn_lo_ready, 1)

            normalise_x(0)
            normalise_x(1)
            remainder_x(0)
            normalise_x(2)
            remainder_x(1)
            split(0, 0)
            split(1, 1)
            normalise_x(3)
            remainder_x(2)
            split(2, 2)
            split(3, 3)
            remainder_x(3)
            normalise_x(4)
            normalise_x(5)
            remainder_x(4)
            normalise_x(6)
            remainder_x(5)
            normalise_x(7)
            remainder_x(6)
            remainder_x(7)
            dve.wait_ge(taps_turned, 1)
            dve.tensor_copy(taps[:, :, :].rearrange("p t g -> p (t g)"), banks[:, 7, 0:(TAPS + 1) * GROUPS]
                            ).then_inc(taps_copied, 1)
            dve.wait_ge(taps_turned, 2)
            dve.tensor_copy(rel_tab, banks[0:HEADS, 6, 0:REL]).then_inc(rel_copied, 1)
            dve.wait_ge(x_turned, 4 * ST)
            dve.wait_ge(x_squared, ST)
            dve.memset(u_buf[:, 0:2], 0.0).then_inc(u_zeroed, 1)
            for kv in range(KVH):
                dve.memset(logits[kv][:, :, 0:CHUNK], NEG).then_inc(neg_written, 1)
            dve.wait_ge(small_loaded, 16 * 7)
            for kv in range(KVH):
                for par in range(2):
                    rows = slice(par * CHUNK, (par + 1) * CHUNK)
                    sink = sink_row[rows, :].rearrange("p (v j a) -> p v j a", v=KVH, a=2)[:, kv, :, par]
                    dve.tensor_copy(logits[kv][rows, :, BAND], sink).then_inc(sinks_placed, 1)

            def stage_lo(tile, par):
                dve.wait_ge(hi_staged, tile + 1)
                dve.tensor_tensor(stage[:, 1, :].bitcast(F32R).rearrange("p (a s) -> p a s", a=2),
                                  proj[par], stage[:, 0, :].rearrange("p (a s) -> p a s", a=2), ALU.subtract
                                  ).then_inc(proj_free, 1)

            def silu(out_ap, count, par):
                dve.wait_ge(gate_exp, count)
                dve.tensor_scalar(h_buf, h_buf, 1.0, None, ALU.add).then_inc(gate_divisor, 1)
                dve.wait_ge(gate_divisor, count)
                dve.reciprocal(h_buf, h_buf).then_inc(sigmoid_ready, 1)
                dve.wait_ge(sigmoid_ready, count)
                dve.tensor_tensor(out_ap.rearrange("p (a s) -> p a s", a=2), proj[par],
                                  h_buf.rearrange("p (a s) -> p a s", a=2), ALU.mult).then_inc(proj_free, 1)

            def attn_gate(tile, par, first=False):
                if not first:
                    dve.wait_ge(gate_stored, (tile - QKV_TILES) * 16)
                silu(y_buf, tile - (QKV_TILES - 1), par)

            def splits(e, middle=None):
                split(e * 4 + 3, 3)
                if middle:
                    middle()
                for q in range(3):
                    split(e * 4 + 4 + q, q)

            for q in range(3):
                split(4 + q, q)
            with dve.Fori(0, QKV_TILES // 2) as i:
                for par in range(2):
                    splits(i * 2 + (1 + par), lambda: stage_lo(i * 2 + par, par))

            def gate_pair(i, first):
                for par in range(2):
                    splits(i * 2 + (1 + par), lambda: attn_gate(i * 2 + par, par, first and par == 0))

            gate_pair(QKV_TILES // 2, True)
            with dve.Fori(QKV_TILES // 2 + 1, A_TILES // 2 - 1) as i:
                gate_pair(i, False)
            splits(A_TILES - 1, lambda: attn_gate(A_TILES - 2, 0))
            dve.wait_ge(bias_loaded, 32)

            def shift_logits(unit, kv, first_chunk):
                dve.wait_ge(qk_done, unit + 1)
                lo = CHUNK if first_chunk else 0
                dve.scalar_tensor_tensor(out=logits[kv][:, :, lo:BAND], in0=logit_ps[:, :, 1, lo:],
                                         scalar=SCALE, in1=bias[:, kv * PAIRS:(kv + 1) * PAIRS, lo:],
                                         op0=ALU.mult, op1=ALU.add).then_inc(logits_read, 1)
                dve.wait_ge(logits_read, unit * 2 + 1)
                dve.scalar_tensor_tensor(out=logits[kv][:, :, lo:BAND], in0=logit_ps[:, :, 0, lo:],
                                         scalar=SCALE, in1=logits[kv][:, :, lo:BAND],
                                         op0=ALU.mult, op1=ALU.add).then_inc(logits_read, 1)
                dve.wait_ge(logits_read, unit * 2 + 2)
                if first_chunk:
                    dve.wait_ge(neg_written, KVH)
                    dve.wait_ge(sinks_placed, 2 * KVH)
                dve.tensor_reduce(row_max, logits[kv], AX_X, ALU.max).then_inc(max_ready, 1)
                dve.wait_ge(max_ready, unit + 1)
                if not (isinstance(unit, int) and unit == 0):
                    dve.wait_ge(probs_turned, unit)
                dve.tensor_tensor(probs, logits[kv], row_max.unsqueeze(2).to_broadcast([P, PAIRS, LW]),
                                  ALU.subtract).then_inc(shifted, 1)

            def normalise(unit):
                dve.wait_ge(exp_done, unit + 1)
                dve.tensor_reduce(row_sum, probs, AX_X, ALU.add).then_inc(sum_ready, 1)
                dve.wait_ge(sum_ready, unit + 1)
                dve.reciprocal(row_inv, row_sum).then_inc(inv_ready, 1)
                dve.wait_ge(inv_ready, unit + 1)
                dve.tensor_tensor(probs[:, :, 0:BAND], probs[:, :, 0:BAND],
                                  row_inv.unsqueeze(2).to_broadcast([P, PAIRS, BAND]), ALU.mult
                                  ).then_inc(probs_ready, 1)

            def gate_output(unit, first):
                dve.wait_ge(o_lo_ready, unit + 1)
                if not first:
                    dve.wait_ge(o_stored, unit * 16)
                for par in range(2):
                    rows = slice(par * HEAD, (par + 1) * HEAD)
                    op = dve.tensor_tensor(o_mix[rows, :, :], o_ps[rows, par, :, :], o_lo[rows, :, :], ALU.add)
                op.then_inc(o_summed, 1)
                dve.wait_ge(o_summed, unit + 1)
                dve.wait_ge(g_loaded, unit * 16 + 16)
                dve.tensor_tensor(o_mix, o_mix, g_cur, ALU.mult).then_inc(o_ready, 1)

            def halves(ap):
                return ap.rearrange("p (a s) -> p a s", a=2)

            def conv_h(g, e):
                dve.wait_ge(w_free, e * 4 + 8)
                dve.tensor_copy(halves(h_buf), proj[0]).then_inc(proj_free, 1)

            def conv_c(g, e, first):
                dve.wait_ge(w_free, e * 4 + 8)
                dve.wait_ge(proj_free, e + 2)
                dve.tensor_tensor(halves(u_buf[:, 2:]), proj[1], halves(h_buf), ALU.mult).then_inc(proj_free, 1)
                dve.wait_ge(proj_free, e + 3)
                if first:
                    dve.wait_ge(gate_stored, 16 * (A_TILES - QKV_TILES))
                    dve.wait_ge(u_zeroed, 1)
                else:
                    dve.wait_ge(conv_stored, g * 16)
                dve.tensor_scalar(y_buf, u_buf[:, 2:2 + S], tap_ap(2, g), tap_ap(3, g), ALU.mult, ALU.add
                                  ).then_inc(conv_step, 1)
                for t in (1, 0):
                    dve.wait_ge(conv_step, g * 4 + 2 - t)
                    dve.scalar_tensor_tensor(out=y_buf, in0=u_buf[:, t:t + S], scalar=tap_ap(t, g), in1=y_buf,
                                             op0=ALU.mult, op1=ALU.add).then_inc(conv_step, 1)

            def tap_ap(t, g):
                return taps[:, t, bass.ds(g, 1)]

            def conv_gate(g, e):
                dve.wait_ge(conv_step, g * 4 + 3)
                silu(u_buf[:, 2:], g + (A_TILES - QKV_TILES + 1), 0)
                dve.wait_ge(proj_free, e + 3)
                dve.tensor_tensor(y_buf, y_buf, u_buf[:, 2:], ALU.mult).then_inc(conv_step, 1)

            def conv_b_gate(g, e):
                dve.wait_ge(w_free, e * 4 + 8)
                dve.wait_ge(conv_step, g * 4 + 4)
                dve.tensor_tensor(halves(y_buf), proj[1], halves(y_buf), ALU.mult).then_inc(proj_free, 1)

            def mix_lo(t):
                dve.wait_ge(mix_hi_ready, t + 1)
                dve.tensor_tensor(act_lo[:, t, 0:N], mix_raw[t % MR], act_hi[:, t, 0:N], ALU.subtract
                                  ).then_inc(mix_lo_ready, 1)

            def mix2_lo(t):
                dve.wait_ge(mix_hi_ready, KT + t + 1)
                dve.tensor_tensor(act_lo[:, t, N:], late_raw[t % LR], act_hi[:, t, N:], ALU.subtract
                                  ).then_inc(mix_lo_ready, 1)

            def tail_split(k):
                dve.wait_ge(tail_hi_ready, k + 1)
                dve.tensor_tensor(tail_lo[:, k, :], late_raw[k % LR], tail_hi[:, k, :], ALU.subtract
                                  ).then_inc(tail_lo_ready, 1)

            def group(g, first, last):
                for kind in range(4):
                    e = g * 4 + A_TILES + kind
                    unit = g * 4 + kind
                    shift_logits(unit, kind % 2, first and kind < 2)
                    if not (first and kind == 0):
                        gate_output(unit - 1, first and kind == 1)
                    split(e * 4 + 3, 3)
                    normalise(unit)
                    split(e * 4 + 4, 0)
                    if kind == 0:
                        if first:
                            attn_gate(A_TILES - 1, 1)
                        else:
                            conv_b_gate(g - 1, e - 1)
                    elif kind == 1:
                        conv_h(g, e - 1)
                    elif kind == 2:
                        conv_c(g, e - 1, first)
                    else:
                        conv_gate(g, e - 1)
                    dve.wait_ge(pt_hi_ready, unit + 1)
                    dve.tensor_tensor(pt_lo[:, :], pt_ps, pt_hi[:, :], ALU.subtract).then_inc(pt_lo_ready, 1)
                    split(e * 4 + 5, 1)
                    split(e * 4 + 6, 2)
                    if last and kind == 3:
                        for t in range(3):
                            mix_lo(t)

            group(0, True, False)
            with dve.Fori(1, GROUPS - 1) as g:
                group(g, False, False)
            group(GROUPS - 1, False, True)

            gate_output(UNITS - 1, False)
            conv_b_gate(GROUPS - 1, TILES - 1)

            def add_resid(r):
                b, st = r // 4, r % 4
                if st < 3 or b == BLOCKS - 1:
                    dve.wait_ge(out_done, 3 * b + st + 1)
                else:
                    dve.wait_ge(w_free, WO_Q + 4 + (b + 1) * KT)
                dve.wait_ge(resid_loaded[r % 2], 16 * (r // 2 + 1))
                if r == 0:
                    dve.wait_ge(conv_stored, 16 * GROUPS)
                    dve.wait_ge(o_stored, 16 * UNITS)
                if r == 16:
                    dve.wait_ge(out_stored, 16 * 4)
                dve.tensor_tensor(y_res[:, st, (b % 4) * N:(b % 4 + 1) * N], banks[:, 4 - 4 * (b % 2) + st, :],
                                  resid[:, r % 2, :], ALU.add).then_inc(y_ready, 1)

            def final_rstd(count, squared, rows):
                dve.wait_ge(bank_free, 8 + squared)
                dve.tensor_reduce(y_ssq[:, rows], ssq[:, rows, :], AX_X, ALU.add).then_inc(y_ssq_ready, 1)
                dve.wait_ge(y_ssq_ready, count)
                dve.tensor_scalar(y_var[:, rows], y_ssq[:, rows], 1.0 / D, EPS, ALU.mult, ALU.add
                                  ).then_inc(y_var_ready, 1)
                dve.wait_ge(y_rstd_ready, count)

            for b in range(BLOCKS):
                for k in range(KT):
                    piece = b * KT + k + 3
                    if piece < RING_PIECES:
                        split(WO_Q + piece, piece % 4)
                    if b == 0 and k + 3 < KT:
                        mix_lo(k + 3)
                    step = (b - 1) * KT + k
                    if step % 2 == 1 and 3 <= step < 2 * KT + 3:
                        mix2_lo((step - 3) // 2)
                    step = (b - 5) * KT + k
                    if step % 2 == 1 and 3 <= step < 2 * KT + 3:
                        tail_split((step - 3) // 2)
                    if b > 0 and k < 4:
                        add_resid(4 * (b - 1) + k)
                    if b == 4 and 4 <= k < 8:
                        st = k - 4
                        if st == 0:
                            final_rstd(1, 16, slice(0, 4))
                            dve.wait_ge(y_weighted, 16)
                        dve.tensor_scalar(y_res[:, st, :], y_res[:, st, :], y_rstd[:, st:st + 1], None, ALU.mult
                                          ).then_inc(y_final, 1)
            dve.wait_ge(final_row_loaded, 16)
            for st in range(4):
                add_resid(4 * (BLOCKS - 1) + st)
                final_rstd(2 + st, 16 + 12 + st + 1, slice(st, st + 1))
                dve.wait_ge(y_weighted, 28)
                dve.tensor_scalar(y_res[:, st, 2 * N:3 * N], y_res[:, st, 2 * N:3 * N], y_rstd[:, st:st + 1], None,
                                  ALU.mult)
                dve.scalar_tensor_tensor(out=y_res[:, st, 3 * N:], in0=y_res[:, st, 3 * N:],
                                         scalar=y_rstd[:, st:st + 1], in1=final_row[:, 3 * N:],
                                         op0=ALU.mult, op1=ALU.mult).then_inc(y_final, 1)

        @block.tensor
        def _(pe):
            def turn_x(t):
                pe.wait_ge(x_normed, t + 1)
                for b in range(4):
                    earlier = [i for i in range(4 * t + b) if TURN_BANKS[i] == turn_bank(t, b)]
                    if earlier:
                        pe.wait_ge(hn_lo_ready, earlier[-1] + 1)
                    for j in range(4):
                        k = 4 * b + j
                        op = pe.transpose(banks[:, turn_bank(t, b), j * P:(j + 1) * P],
                                          x_tile[t % XR][:, k * P:(k + 1) * P], ident[:, :])
                    op.then_inc(x_turned, 1)

            def quarter(q, count, par, spans=((0, N), (N, S))):
                pe.wait_ge(w_lo_ready, count + 1)
                for j in range(QK):
                    k = q * QK + j
                    wh = w_hi[:, q, j * P:(j + 1) * P]
                    wl = w_lo[:, q, j * P:(j + 1) * P]
                    for w, a in ((wh, act_hi), (wh, act_lo), (wl, act_hi)):
                        for lo, hi in spans:
                            op = pe.matmul(proj[par][:, lo // N, lo % N:lo % N + hi - lo], w, a[:, k, lo:hi],
                                           start=(k == 0 and w is wh and a is act_hi),
                                           stop=(k == KT - 1 and w is wl))
                return op

            def first_tile(q, part):
                return quarter(q, q, 0, ((part * S // 4, (part + 1) * S // 4),))

            pe.wait_ge(ident_ready, 1)
            for t in range(3):
                turn_x(t)
            pe.wait_ge(proj_free, 1)
            pe.wait_ge(hn_lo_ready, 4 * 2)
            first_tile(0, 0)
            first_tile(1, 0)
            turn_x(3)
            first_tile(2, 0)
            first_tile(3, 0)
            pe.wait_ge(hn_lo_ready, 4 * 4)
            for q in range(3):
                first_tile(q, 1)
                turn_x(4 + q)
            first_tile(3, 1)
            pe.wait_ge(hn_lo_ready, 4 * 6)
            first_tile(0, 2)
            first_tile(1, 2)
            turn_x(7)
            first_tile(2, 2)
            first_tile(3, 2)
            pe.wait_ge(hn_lo_ready, 4 * ST)
            pe.wait_ge(small_loaded, 16 * 7)
            rows = (TAPS + 1) * GROUPS
            pe.transpose(banks[:, 7, 0:rows], tap_rows, ident[0:rows, 0:rows]).then_inc(taps_turned, 1)
            pe.matmul(banks[0:HEADS, 6, 0:REL], rel_rows, hot_rows, start=True, stop=True
                      ).then_inc(taps_turned, 1)
            for q in range(4):
                first_tile(q, 3).then_inc(w_free, 1)

            def column_tile(i, par):
                pe.wait_ge(proj_free, i * 2 + (par + 1))
                for q in range(4):
                    quarter(q, i * 8 + (4 * par + q), par).then_inc(w_free, 1)

            column_tile(0, 1)
            with pe.Fori(1, A_TILES // 2) as i:
                for par in range(2):
                    column_tile(i, par)

            with pe.Fori(0, GROUPS) as g:
                for kind in range(4):
                    e = g * 4 + (A_TILES + kind)
                    unit = g * 4 + kind
                    kv = kind % 2
                    pe.wait_ge(qk_loaded, unit * 64 + 64)
                    for j in range(PAIRS):
                        op = pe.matmul(logit_ps[:, j, :, :].rearrange("p c k -> p (c k)"),
                                       q_cur[:, 2 * j:2 * j + 2, :].rearrange("p h s -> p (h s)"),
                                       k_cur[:, :, :].rearrange("p c k -> p (c k)"), start=True, stop=True)
                    op.then_inc(qk_done, 1)
                    pe.wait_ge(proj_free, e + 1)
                    quarter(0, e * 4, kind % 2).then_inc(w_free, 1)
                    if kv == 0:
                        pe.wait_ge(v_loaded, (g * 2 + kind // 2) * 16 + 16)
                        for c in range(2):
                            op = pe.transpose(v_ps[:, c * P:(c + 1) * P], v_win[:, c, :], ident[:, :])
                        op.then_inc(v_turned, 1)
                    quarter(1, e * 4 + 1, kind % 2).then_inc(w_free, 1)
                    pe.wait_ge(probs_ready, unit + 1)
                    for j in range(PAIRS):
                        op = pe.transpose(pt_ps[:, j * P:(j + 1) * P], probs[:, j, 0:BAND], ident[:, :])
                    op.then_inc(probs_turned, 1)
                    quarter(2, e * 4 + 2, kind % 2).then_inc(w_free, 1)
                    quarter(3, e * 4 + 3, kind % 2).then_inc(w_free, 1)
                    pe.wait_ge(pt_lo_ready, unit + 1)
                    pe.wait_ge(v_ready, g * 2 + (kind // 2 + 1))
                    for par in range(2):
                        v_pair = v_cur[:, kv, par:par + 2, :].rearrange("p a d -> p (a d)")
                        for i, pt in enumerate((pt_hi, pt_lo)):
                            heads = pt[:, :].rearrange("p (j a k) -> p j a k", j=PAIRS, a=2)[:, :, par, :]
                            op = pe.matmul(o_ps[:, par, :, :], v_pair, heads, start=(i == 0), stop=(i == 1))
                    op.then_inc(pv_done, 1)

            def out_block(b, par, half):
                first = half == 0
                for k in range(KT):
                    pe.wait_ge(w_lo_ready, b * KT + (WO_Q + k + 1))
                    pe.wait_ge(mix_lo_ready, half * KT + k + 1)
                    for st in range(4):
                        tok = slice(half * N + st * P, half * N + (st + 1) * P)
                        if k == 0:
                            pe.wait_ge(bank_free, b * 4 + (st + 1))
                            if first and par == 0 and st == 0:
                                pe.wait_ge(v_ready, NC)
                            if first and par == 0 and st == 3:
                                pe.wait_ge(o_ready, UNITS)
                            if first and par == 1 and st == 0:
                                pe.wait_ge(proj_free, TILES + 2)
                        bank = banks[:, 4 - 4 * par + st, :]
                        for i, (a, w) in enumerate(((act_hi, w_hi), (act_hi, w_lo), (act_lo, w_hi))):
                            op = pe.matmul(bank, a[:, k, tok], w[:, k % 4, :], start=(k == 0 and i == 0),
                                           stop=(k == KT - 1 and i == 2))
                        if k == KT - 1 and st < 3:
                            op.then_inc(out_done, 1)
                    op.then_inc(w_free, 1)

            with pe.Fori(0, 2) as i:
                for par in range(2):
                    out_block(i * 2 + par, par, 0)
            for b in range(4, BLOCKS - 1):
                out_block(b, b % 2, 1)
            for st in range(4):
                pe.wait_ge(bank_free, (BLOCKS - 1) * 4 + st + 1)
                tok = slice(N + st * P, N + (st + 1) * P)
                for k in range(KT):
                    if st == 0:
                        pe.wait_ge(tail_lo_ready, k + 1)
                    for i, (a, w) in enumerate(((act_hi, tail_hi), (act_hi, tail_lo), (act_lo, tail_hi))):
                        op = pe.matmul(banks[:, st, :], a[:, k, tok], w[:, k, :], start=(k == 0 and i == 0),
                                       stop=(k == KT - 1 and i == 2))
                op.then_inc(out_done, 1)


_INS = ["x", "norm_w", "w_in", "sinks", "conv_w", "conv_b", "w_out", "rel_bias", "final_norm_w"]


def kernel(**inputs):
    import numpy as _np
    import concourse.bacc as _bacc
    from concourse import mybir as _mybir
    from concourse.bass_utils import run_bass_kernel_spmd as _run

    nc = _bacc.Bacc("TRN2", target_bir_lowering=False, num_devices=1)
    given = {name: _np.ascontiguousarray(inputs[name]) for name in _INS}
    given["one_hot"] = t5_one_hot()
    arrays, args = {}, []
    for name, a in given.items():
        arrays[f"in_{name}_dram"] = a
        args.append(nc.dram_tensor(f"in_{name}_dram", a.shape, _mybir.dt.from_np(a.dtype), kind="ExternalInput").ap())
    args.append(nc.dram_tensor("out_0_dram", (1, S, D), F32, kind="ExternalOutput").ap())
    build(nc, *args)
    r = _run(nc, [arrays], core_ids=[0])
    return r.results[0]["out_0_dram"]
```
